# Optimizing a Trainium2 kernel written in Bass

```python
import math
import jax, jax.numpy as jnp
from jax import lax
import numpy as np

D_MODEL = 1024
BATCH = 1
SEQ = 256
DEPTH = 2

GRID_W = 64
HEAD_DIM = 128
ATTN_WIDTH = D_MODEL
N_HEADS = ATTN_WIDTH // HEAD_DIM
N_KV_HEADS = 2
GROUP = N_HEADS // N_KV_HEADS
KV_WIDTH = N_KV_HEADS * HEAD_DIM
Q_BLOCK = 128
ROPE_THETA = 10000.0
ROPE_HALF = HEAD_DIM // 2
POOL_WINDOWS = (2, 4, 8, 16)
N_POOL_GROUPS = 4
POOL_WIDTH = D_MODEL // 2
POOL_GROUP_DIM = POOL_WIDTH // N_POOL_GROUPS
IN_COLS = ATTN_WIDTH + 2 * KV_WIDTH + POOL_WIDTH + 2 * D_MODEL
N_PEER_HEADS = 8
PEER_QUERY_DIM = 512
SUBKEY_DIM = PEER_QUERY_DIM // 2
N_KEYS = 128
N_EXPERTS = N_KEYS * N_KEYS
PEER_TOPK = 16
TOKEN_BLOCK = 128
N_ADA = 6
EPS = 1e-6


def rms_norm(x, w):
    xf = x.astype(jnp.float32)
    y = xf * lax.rsqrt(jnp.mean(xf * xf, axis=-1, keepdims=True) + EPS)
    return (y * w.astype(jnp.float32)).astype(x.dtype)

def modulate(xn, shift, scale):
    return xn * (1.0 + scale[:, None, :]) + shift[:, None, :]

def axial_rope_angles(seq_len):
    rows = seq_len // GRID_W
    t = jnp.arange(rows * GRID_W)
    row = (t // GRID_W).astype(jnp.float32)
    col = (t % GRID_W).astype(jnp.float32)
    inv = 1.0 / (ROPE_THETA ** (jnp.arange(0, ROPE_HALF, 2, dtype=jnp.float32) / ROPE_HALF))
    return row[:, None] * inv, col[:, None] * inv

def rotate_half_dims(xh, ang):
    half = ROPE_HALF // 2
    cos = jnp.cos(ang)[None, :, None, :]
    sin = jnp.sin(ang)[None, :, None, :]
    xf = xh.astype(jnp.float32)
    x1, x2 = xf[..., :half], xf[..., half:]
    return jnp.concatenate([x1 * cos - x2 * sin, x2 * cos + x1 * sin], axis=-1).astype(xh.dtype)

def apply_axial_rope(x, ang_r, ang_c):
    return jnp.concatenate([rotate_half_dims(x[..., :ROPE_HALF], ang_r),
                            rotate_half_dims(x[..., ROPE_HALF:], ang_c)], axis=-1)

def blocked_bidirectional_gqa(q, k, v):
    B, S = q.shape[0], q.shape[1]
    nb = S // Q_BLOCK
    scale = 1.0 / math.sqrt(HEAD_DIM)
    qb = q.reshape(B, nb, Q_BLOCK, N_KV_HEADS, GROUP, HEAD_DIM).swapaxes(0, 1)

    def one_block(qblk):
        s = jnp.einsum('bqkgd,bskd->bkgqs', qblk, k).astype(jnp.float32) * scale
        p = jax.nn.softmax(s, axis=-1).astype(v.dtype)
        return jnp.einsum('bkgqs,bskd->bqkgd', p, v)

    ob = lax.map(one_block, qb)
    return ob.swapaxes(0, 1).reshape(B, S, N_HEADS * HEAD_DIM)

def multiscale_pool(u, pool_mix_w, pool_scale):
    B, S, _ = u.shape
    ug = u.reshape(B, S, N_POOL_GROUPS, POOL_GROUP_DIM).astype(jnp.float32)
    t = jnp.arange(S)
    outs = []
    for gi, w in enumerate(POOL_WINDOWS):
        xg = ug[:, :, gi, :]
        csum = jnp.concatenate([jnp.zeros((B, 1, POOL_GROUP_DIM), jnp.float32),
                                jnp.cumsum(xg, axis=1)], axis=1)
        lo = jnp.clip(t - w // 2, 0, S)
        hi = jnp.clip(t + w // 2, 0, S)
        cnt = (hi - lo).astype(jnp.float32)[None, :, None]
        outs.append((csum[:, hi] - csum[:, lo]) / cnt - xg)
    m = jnp.stack(outs, axis=2).astype(u.dtype)
    mixed = jnp.einsum('bsgc,gcd->bsgd', m, pool_mix_w).reshape(B, S, POOL_WIDTH)
    return mixed * pool_scale

def peer_ffn(xm, w_query, sub_keys, expert_u, expert_v):
    B, S, D = xm.shape
    nb = S // TOKEN_BLOCK
    xb = xm.reshape(B, nb, TOKEN_BLOCK, D).swapaxes(0, 1)

    def one_block(xblk):
        q = (xblk @ w_query).reshape(B, TOKEN_BLOCK, N_PEER_HEADS, 2, SUBKEY_DIM)
        s = jnp.einsum('bthpd,hpnd->bthpn', q, sub_keys).astype(jnp.float32)
        vals, idx = lax.top_k(s, PEER_TOPK)
        cand = (vals[..., 0, :, None] + vals[..., 1, None, :]).reshape(B, TOKEN_BLOCK, N_PEER_HEADS, PEER_TOPK * PEER_TOPK)
        cand_idx = (idx[..., 0, :, None] * N_KEYS + idx[..., 1, None, :]).reshape(B, TOKEN_BLOCK, N_PEER_HEADS, PEER_TOPK * PEER_TOPK)
        top_s, pos = lax.top_k(cand, PEER_TOPK)
        eidx = jnp.take_along_axis(cand_idx, pos, axis=-1)
        g = jax.nn.softmax(top_s, axis=-1).astype(xblk.dtype)
        u = expert_u[eidx]
        h = jnp.einsum('btd,bthkd->bthk', xblk, u)
        act = jax.nn.gelu(h, approximate=False) * g
        return jnp.einsum('bthk,bthkd->btd', act, expert_v[eidx])

    yb = lax.map(one_block, xb)
    return yb.swapaxes(0, 1).reshape(B, S, D)

def first_inputs(seed: int = 0) -> dict:
    key = jax.random.key(seed)
    ks = jax.random.split(key, 20)
    f32 = jnp.float32
    nrm = lambda k, shape, s: (jax.random.normal(k, shape, f32) * s)
    return {
        "x": nrm(ks[0], (BATCH, SEQ, D_MODEL), 1.0),
        "c": nrm(ks[1], (BATCH, D_MODEL), 1.0),
        "ada_w": nrm(ks[2], (DEPTH, D_MODEL, N_ADA * D_MODEL), 0.5 * D_MODEL ** -0.5),
        "ada_b": nrm(ks[3], (DEPTH, N_ADA * D_MODEL), 0.01),
        "norm_mix_w": 1.0 + nrm(ks[4], (DEPTH, D_MODEL), 0.05),
        "w_in": nrm(ks[5], (DEPTH, D_MODEL, IN_COLS), D_MODEL ** -0.5),
        "q_norm_w": 1.0 + nrm(ks[6], (DEPTH, HEAD_DIM), 0.05),
        "k_norm_w": 1.0 + nrm(ks[7], (DEPTH, HEAD_DIM), 0.05),
        "w_attn_o": nrm(ks[8], (DEPTH, ATTN_WIDTH, D_MODEL), ATTN_WIDTH ** -0.5),
        "pool_mix_w": nrm(ks[9], (DEPTH, N_POOL_GROUPS, POOL_GROUP_DIM, POOL_GROUP_DIM), POOL_GROUP_DIM ** -0.5),
        "pool_scale": 1.0 + nrm(ks[10], (DEPTH, POOL_WIDTH), 0.05),
        "w_pool_o": nrm(ks[11], (DEPTH, POOL_WIDTH, D_MODEL), POOL_WIDTH ** -0.5),
        "w_out": nrm(ks[12], (DEPTH, D_MODEL, D_MODEL), D_MODEL ** -0.5),
        "norm_ffn_w": 1.0 + nrm(ks[13], (DEPTH, D_MODEL), 0.05),
        "w_query": nrm(ks[14], (DEPTH, D_MODEL, N_PEER_HEADS * PEER_QUERY_DIM), D_MODEL ** -0.5),
        "sub_keys": nrm(ks[15], (DEPTH, N_PEER_HEADS, 2, N_KEYS, SUBKEY_DIM), SUBKEY_DIM ** -0.5),
        "expert_u": nrm(ks[16], (DEPTH, N_EXPERTS, D_MODEL), D_MODEL ** -0.5),
        "expert_v": nrm(ks[17], (DEPTH, N_EXPERTS, D_MODEL), N_PEER_HEADS ** -0.5),
        "final_norm_w": 1.0 + nrm(ks[18], (D_MODEL,), 0.05),
    }

def first_block(x, c, ada_w, ada_b, norm_mix_w, w_in, q_norm_w, k_norm_w, w_attn_o, pool_mix_w,
              pool_scale, w_pool_o, w_out, norm_ffn_w, w_query, sub_keys, expert_u, expert_v,
              final_norm_w):
    B, S, _ = x.shape
    ang_r, ang_c = axial_rope_angles(S)
    c_act = jax.nn.silu(c)
    splits = [ATTN_WIDTH, ATTN_WIDTH + KV_WIDTH, ATTN_WIDTH + 2 * KV_WIDTH,
              ATTN_WIDTH + 2 * KV_WIDTH + POOL_WIDTH, ATTN_WIDTH + 2 * KV_WIDTH + POOL_WIDTH + D_MODEL]
    for l in range(DEPTH):
        mod = c_act @ ada_w[l] + ada_b[l]
        sh1, sc1, g1, sh2, sc2, g2 = jnp.split(mod, N_ADA, axis=-1)

        xm = modulate(rms_norm(x, norm_mix_w[l]), sh1, sc1)
        proj = xm @ w_in[l]
        q, k, v, u_pool, ga, gp = jnp.split(proj, splits, axis=-1)

        q = rms_norm(q.reshape(B, S, N_HEADS, HEAD_DIM), q_norm_w[l])
        k = rms_norm(k.reshape(B, S, N_KV_HEADS, HEAD_DIM), k_norm_w[l])
        v = v.reshape(B, S, N_KV_HEADS, HEAD_DIM)
        q = apply_axial_rope(q, ang_r, ang_c).reshape(B, S, N_KV_HEADS, GROUP, HEAD_DIM)
        k = apply_axial_rope(k, ang_r, ang_c)
        attn = blocked_bidirectional_gqa(q, k, v) @ w_attn_o[l]

        pool = multiscale_pool(u_pool, pool_mix_w[l], pool_scale[l]) @ w_pool_o[l]

        merged = jax.nn.sigmoid(ga) * attn + jax.nn.sigmoid(gp) * pool
        x = x + g1[:, None, :] * (merged @ w_out[l])

        xf = modulate(rms_norm(x, norm_ffn_w[l]), sh2, sc2)
        x = x + g2[:, None, :] * peer_ffn(xf, w_query[l], sub_keys[l], expert_u[l], expert_v[l])

    return rms_norm(x, final_norm_w)


D_FF = 2816
SSD_EXPAND = 2
SSD_D_INNER = SSD_EXPAND * D_MODEL
SSD_HEAD_DIM = 64
SSD_HEADS = SSD_D_INNER // SSD_HEAD_DIM
SSD_GROUPS = 4
SSD_HPG = SSD_HEADS // SSD_GROUPS
SSD_STATE = 128
SSD_CONV = 4
SSD_CHUNK = 128
SSD_CONV_DIM = SSD_D_INNER + 2 * SSD_GROUPS * SSD_STATE
MLA_HEADS = 8
MLA_Q_LORA = 512
MLA_KV_LORA = 256
MLA_NOPE = 128
MLA_ROPE = 64
MLA_V = 128
MLA_QK = MLA_NOPE + MLA_ROPE
ATTN_BLOCK = 128
IN_SPLIT_SIZES = (SSD_D_INNER, SSD_CONV_DIM, SSD_HEADS, MLA_Q_LORA, MLA_KV_LORA, MLA_ROPE, 2 * D_MODEL)
D_IN_PROJ = SSD_D_INNER + SSD_CONV_DIM + SSD_HEADS + MLA_Q_LORA + MLA_KV_LORA + MLA_ROPE + 2 * D_MODEL


def rms_norm_2(x, g):
    xf = x.astype(jnp.float32)
    y = xf * lax.rsqrt(jnp.mean(xf * xf, axis=-1, keepdims=True) + EPS)
    return (y * g.astype(jnp.float32)).astype(x.dtype)

def swiglu(x, w13, w2):
    gu = x @ w13
    gate, up = gu[..., :D_FF], gu[..., D_FF:]
    return (jax.nn.silu(gate) * up) @ w2

def split_cols(t, sizes):
    out, start = [], 0
    for n in sizes:
        out.append(t[..., start:start + n])
        start += n
    return out

def rope_tables(positions):
    inv = 1.0 / (ROPE_THETA ** (jnp.arange(0, MLA_ROPE, 2, dtype=jnp.float32) / MLA_ROPE))
    ang = positions.astype(jnp.float32)[..., None] * inv
    return jnp.cos(ang), jnp.sin(ang)

def apply_rope(t, cos, sin):
    half = MLA_ROPE // 2
    tf = t.astype(jnp.float32)
    t1, t2 = tf[..., :half], tf[..., half:]
    c, s = cos[:, :, None, :], sin[:, :, None, :]
    return jnp.concatenate([t1 * c - t2 * s, t2 * c + t1 * s], axis=-1).astype(t.dtype)

def causal_depthwise_conv(t, w, b):
    y = lax.conv_general_dilated(
        t, w[:, None, :].astype(t.dtype), window_strides=(1,), padding=[(SSD_CONV - 1, 0)],
        dimension_numbers=('NWC', 'WIO', 'NWC'), feature_group_count=t.shape[-1])
    return y + b.astype(t.dtype)

def ssd_chunked_scan(xh, dt, a, bmat, cmat):
    bsz, s = xh.shape[0], xh.shape[1]
    nc = s // SSD_CHUNK

    def chunks(t):
        t = t.reshape((bsz, nc, SSD_CHUNK) + t.shape[2:])
        return jnp.moveaxis(t, 1, 0)

    x_c = chunks(xh.astype(jnp.float32).reshape(bsz, s, SSD_GROUPS, SSD_HPG, SSD_HEAD_DIM))
    dt_c = chunks(dt.reshape(bsz, s, SSD_GROUPS, SSD_HPG))
    b_c = chunks(bmat.astype(jnp.float32))
    c_c = chunks(cmat.astype(jnp.float32))
    a_g = a.reshape(SSD_GROUPS, SSD_HPG)
    causal = jnp.tril(jnp.ones((SSD_CHUNK, SSD_CHUNK), dtype=bool))[None, :, :, None, None]

    def step(state, inp):
        xc, dtc, bc, cc = inp
        acum = jnp.cumsum(dtc * a_g, axis=1)
        seg = acum[:, :, None] - acum[:, None, :]
        decay = jnp.exp(jnp.where(causal, seg, -jnp.inf))
        cb = jnp.einsum('btgn,bsgn->btsg', cc, bc)
        xdt = xc * dtc[..., None]
        y_diag = jnp.einsum('btsg,btsgh,bsghp->btghp', cb, decay, xdt)
        y_off = jnp.einsum('btgn,bghpn->btghp', cc, state) * jnp.exp(acum)[..., None]
        last = acum[:, -1]
        w_state = jnp.exp(last[:, None] - acum)
        new_state = (state * jnp.exp(last)[..., None, None]
                     + jnp.einsum('bsgn,bsgh,bsghp->bghpn', bc, w_state, xdt))
        return new_state, y_diag + y_off

    state0 = jnp.zeros((bsz, SSD_GROUPS, SSD_HPG, SSD_HEAD_DIM, SSD_STATE), jnp.float32)
    _, y = lax.scan(step, state0, (x_c, dt_c, b_c, c_c))
    return jnp.moveaxis(y, 0, 1).reshape(bsz, s, SSD_HEADS, SSD_HEAD_DIM)

def ssd_branch(z, xbc, dt_raw, conv_w, conv_b, dt_bias, a_log, d_skip, norm_g, w_out):
    bsz, s, _ = z.shape
    xbc = jax.nn.silu(causal_depthwise_conv(xbc, conv_w, conv_b))
    xs, bm, cm = split_cols(xbc, (SSD_D_INNER, SSD_GROUPS * SSD_STATE, SSD_GROUPS * SSD_STATE))
    xh = xs.reshape(bsz, s, SSD_HEADS, SSD_HEAD_DIM)
    bm = bm.reshape(bsz, s, SSD_GROUPS, SSD_STATE)
    cm = cm.reshape(bsz, s, SSD_GROUPS, SSD_STATE)
    dt = jax.nn.softplus(dt_raw.astype(jnp.float32) + dt_bias.astype(jnp.float32))
    a = -jnp.exp(a_log.astype(jnp.float32))
    y = ssd_chunked_scan(xh, dt, a, bm, cm) + xh.astype(jnp.float32) * d_skip.astype(jnp.float32)[:, None]
    y = y.reshape(bsz, s, SSD_D_INNER).astype(z.dtype)
    y = rms_norm_2(y * jax.nn.silu(z), norm_g)
    return y @ w_out

def causal_block_attention(q, k, v):
    bsz, s, h, dq = q.shape
    nb = s // ATTN_BLOCK
    scale = dq ** -0.5
    qb = jnp.moveaxis(q.reshape(bsz, nb, ATTN_BLOCK, h, dq), 1, 0)
    kpos = jnp.arange(s)

    def one_block(args):
        i, qi = args
        sc = jnp.einsum('bqhd,bkhd->bhqk', qi, k, preferred_element_type=jnp.float32) * scale
        qpos = i * ATTN_BLOCK + jnp.arange(ATTN_BLOCK)
        sc = jnp.where(kpos[None, :] <= qpos[:, None], sc, -jnp.inf)
        p = jax.nn.softmax(sc, axis=-1)
        return jnp.einsum('bhqk,bkhd->bqhd', p.astype(v.dtype), v)

    o = lax.map(one_block, (jnp.arange(nb), qb))
    return jnp.moveaxis(o, 0, 1).reshape(bsz, s, h, v.shape[-1])

def mla_branch(cq, ckv, kr, cos, sin, q_lora_g, w_uq, kv_lora_g, w_ukv, q_norm_g, k_norm_g, w_out):
    bsz, s, _ = cq.shape
    q = (rms_norm_2(cq, q_lora_g) @ w_uq).reshape(bsz, s, MLA_HEADS, MLA_QK)
    kv = (rms_norm_2(ckv, kv_lora_g) @ w_ukv).reshape(bsz, s, MLA_HEADS, MLA_NOPE + MLA_V)
    k_nope, v = kv[..., :MLA_NOPE], kv[..., MLA_NOPE:]
    k_pe = jnp.broadcast_to(kr[:, :, None, :], (bsz, s, MLA_HEADS, MLA_ROPE))
    k = jnp.concatenate([k_nope, k_pe], axis=-1)
    q = rms_norm_2(q, q_norm_g)
    k = rms_norm_2(k, k_norm_g)
    q = jnp.concatenate([q[..., :MLA_NOPE], apply_rope(q[..., MLA_NOPE:], cos, sin)], axis=-1)
    k = jnp.concatenate([k[..., :MLA_NOPE], apply_rope(k[..., MLA_NOPE:], cos, sin)], axis=-1)
    o = causal_block_attention(q, k, v)
    return o.reshape(bsz, s, MLA_HEADS * MLA_V) @ w_out

def second_inputs(seed: int = 0) -> dict:
    key = jax.random.key(seed)
    ks = jax.random.split(key, 32)
    f32 = jnp.float32

    def nrm(k, shape, fan_in):
        return jax.random.normal(k, shape, f32) * (fan_in ** -0.5)

    def gain(k, n):
        return 1.0 + 0.02 * jax.random.normal(k, (DEPTH, n), f32)

    dt0 = jnp.exp(jax.random.uniform(ks[10], (DEPTH, SSD_HEADS), f32) * (np.log(0.1) - np.log(0.001)) + np.log(0.001))
    dt_bias = dt0 + jnp.log(-jnp.expm1(-dt0))
    a_log = jnp.log(jax.random.uniform(ks[11], (DEPTH, SSD_HEADS), f32, 1.0, 16.0))
    return {
        "x": jax.random.normal(ks[0], (BATCH, SEQ, D_MODEL), f32),
        "positions": jnp.broadcast_to(jnp.arange(SEQ, dtype=jnp.int32)[None, :], (BATCH, SEQ)),
        "ln_ffn1": gain(ks[1], D_MODEL),
        "ffn1_w13": nrm(ks[2], (DEPTH, D_MODEL, 2 * D_FF), D_MODEL),
        "ffn1_w2": nrm(ks[3], (DEPTH, D_FF, D_MODEL), D_FF),
        "ln_mix": gain(ks[4], D_MODEL),
        "w_in": nrm(ks[5], (DEPTH, D_MODEL, D_IN_PROJ), D_MODEL),
        "conv_w": nrm(ks[6], (DEPTH, SSD_CONV, SSD_CONV_DIM), SSD_CONV),
        "conv_b": 0.02 * jax.random.normal(ks[7], (DEPTH, SSD_CONV_DIM), f32),
        "dt_bias": dt_bias,
        "a_log": a_log,
        "d_skip": 1.0 + 0.1 * jax.random.normal(ks[12], (DEPTH, SSD_HEADS), f32),
        "ssd_norm": gain(ks[13], SSD_D_INNER),
        "w_ssd_out": nrm(ks[14], (DEPTH, SSD_D_INNER, D_MODEL), SSD_D_INNER),
        "q_lora_norm": gain(ks[15], MLA_Q_LORA),
        "w_uq": nrm(ks[16], (DEPTH, MLA_Q_LORA, MLA_HEADS * MLA_QK), MLA_Q_LORA),
        "kv_lora_norm": gain(ks[17], MLA_KV_LORA),
        "w_ukv": nrm(ks[18], (DEPTH, MLA_KV_LORA, MLA_HEADS * (MLA_NOPE + MLA_V)), MLA_KV_LORA),
        "q_norm": gain(ks[19], MLA_QK),
        "k_norm": gain(ks[20], MLA_QK),
        "w_mla_out": nrm(ks[21], (DEPTH, MLA_HEADS * MLA_V, D_MODEL), MLA_HEADS * MLA_V),
        "w_o": nrm(ks[22], (DEPTH, D_MODEL, D_MODEL), D_MODEL),
        "ln_ffn2": gain(ks[23], D_MODEL),
        "ffn2_w13": nrm(ks[24], (DEPTH, D_MODEL, 2 * D_FF), D_MODEL),
        "ffn2_w2": nrm(ks[25], (DEPTH, D_FF, D_MODEL), D_FF),
    }

def second_block(x, positions, ln_ffn1, ffn1_w13, ffn1_w2, ln_mix, w_in, conv_w, conv_b, dt_bias,
              a_log, d_skip, ssd_norm, w_ssd_out, q_lora_norm, w_uq, kv_lora_norm, w_ukv,
              q_norm, k_norm, w_mla_out, w_o, ln_ffn2, ffn2_w13, ffn2_w2):
    cos, sin = rope_tables(positions)
    h = x
    for l in range(DEPTH):
        h = h + 0.5 * swiglu(rms_norm_2(h, ln_ffn1[l]), ffn1_w13[l], ffn1_w2[l])
        u = rms_norm_2(h, ln_mix[l])
        z, xbc, dt_raw, cq, ckv, kr, gates = split_cols(u @ w_in[l], IN_SPLIT_SIZES)
        y_ssd = ssd_branch(z, xbc, dt_raw, conv_w[l], conv_b[l], dt_bias[l], a_log[l], d_skip[l],
                           ssd_norm[l], w_ssd_out[l])
        y_mla = mla_branch(cq, ckv, kr, cos, sin, q_lora_norm[l], w_uq[l], kv_lora_norm[l], w_ukv[l],
                           q_norm[l], k_norm[l], w_mla_out[l])
        g = jax.nn.sigmoid(gates.astype(jnp.float32)).astype(h.dtype)
        merged = g[..., :D_MODEL] * y_ssd + g[..., D_MODEL:] * y_mla
        h = h + merged @ w_o[l]
        h = h + 0.5 * swiglu(rms_norm_2(h, ln_ffn2[l]), ffn2_w13[l], ffn2_w2[l])
    return h


def setup_inputs(seed=0):
    out = dict(first_inputs(seed))
    for name, value in second_inputs(seed + 1).items():
        if name != "x":
            out[name + "_2"] = value
    return out


def reference(
    x, c, ada_w, ada_b, norm_mix_w, w_in, q_norm_w, k_norm_w, w_attn_o, pool_mix_w, pool_scale,
    w_pool_o, w_out, norm_ffn_w, w_query, sub_keys, expert_u, expert_v, final_norm_w,
    positions_2, ln_ffn1_2, ffn1_w13_2, ffn1_w2_2, ln_mix_2, w_in_2, conv_w_2, conv_b_2,
    dt_bias_2, a_log_2, d_skip_2, ssd_norm_2, w_ssd_out_2, q_lora_norm_2, w_uq_2,
    kv_lora_norm_2, w_ukv_2, q_norm_2, k_norm_2, w_mla_out_2, w_o_2, ln_ffn2_2, ffn2_w13_2,
    ffn2_w2_2,
):
    x = first_block(
        x, c, ada_w, ada_b, norm_mix_w, w_in, q_norm_w, k_norm_w, w_attn_o, pool_mix_w,
        pool_scale, w_pool_o, w_out, norm_ffn_w, w_query, sub_keys, expert_u, expert_v,
        final_norm_w,
    )
    return second_block(
        x, positions_2, ln_ffn1_2, ffn1_w13_2, ffn1_w2_2, ln_mix_2, w_in_2, conv_w_2, conv_b_2,
        dt_bias_2, a_log_2, d_skip_2, ssd_norm_2, w_ssd_out_2, q_lora_norm_2, w_uq_2,
        kv_lora_norm_2, w_ukv_2, q_norm_2, k_norm_2, w_mla_out_2, w_o_2, ln_ffn2_2, ffn2_w13_2,
        ffn2_w2_2,
    )


_drawn_inputs = setup_inputs


def setup_inputs(seed=0):
    import zlib

    import numpy as np

    out = dict(_drawn_inputs(seed))
    spreads = {}
    factors = {'ada_b': 2.75,
     'q_norm_w': 8.0,
     'k_norm_w': 8.0,
     'pool_scale': 2.896,
     'ln_ffn1_2': 4.095,
     'conv_b_2': 3.06,
     'ssd_norm_2': 4.259,
     'q_lora_norm_2': 8.0,
     'kv_lora_norm_2': 8.0,
     'q_norm_2': 8.0,
     'k_norm_2': 8.0,
     'ln_ffn2_2': 5.426}
    for name, (base, spread) in spreads.items():
        noise = np.random.default_rng([zlib.crc32(name.encode()), seed]).standard_normal(out[name].shape)
        drawn = base * np.exp(spread * noise) if base else spread * noise
        out[name] = __import__('jax').numpy.asarray(drawn.astype(out[name].dtype))
    for name, factor in factors.items():
        out[name] = (out[name] * factor).astype(out[name].dtype)
    return out
```

```python
from contextlib import ExitStack

import numpy as np

import concourse.bass as bass
from concourse import mybir

ALU = mybir.AluOpType
ACT = mybir.ActivationFunctionType
AX_X = mybir.AxisListType.X
F32 = mybir.dt.float32
F32R = mybir.dt.float32r
I32 = mybir.dt.int32
U32 = mybir.dt.uint32

P = 128
S = 256
TT = S // P
D = 1024
KD = D // P
DEPTH = 2
EPS = 1e-6
TILES = 8
RING = 8
RING_2 = 6
PARTS = 3
GB = 4
NEG = -3.0e38

HEADS, KV_HEADS, HEAD_DIM = 8, 2, 128
GROUP = HEADS // KV_HEADS
UNITS = KV_HEADS + HEADS
POOL_WINDOWS = (2, 4, 8, 16)
PADW = 8
PEER_HEADS, N_KEYS, TOPK = 8, 128, 16
N_EXPERTS = N_KEYS * N_KEYS
ROUNDS = PEER_HEADS * TT
SLOTS = 8
N_ADA = 6

T_IN = (2 * KV_HEADS * HEAD_DIM + D + D // 2 + 2 * D) // P
TILES_1 = (N_ADA * KD * KD + T_IN * KD + 4 + 4 * KD + 2 * KD * KD
           + PEER_HEADS * (4 * KD + 4))
CHUNKS_1 = -(-TILES_1 // TILES)

PAR_1 = {}
for _name, _n in (("ada_b", N_ADA * KD), ("norm_mix", KD), ("norm_ffn", KD), ("q_norm", 1),
                  ("k_norm", 1), ("pool_scale", 4)):
    PAR_1[_name] = (sum(n for _, n in PAR_1.values()), _n)
NPAR_1 = sum(n for _, n in PAR_1.values())

G_IN = 0
G_MIX = G_IN + T_IN
G_POOLO = G_MIX + 4
G_ATTO = G_POOLO + KD
G_OUT = G_ATTO + KD
G_XT = G_OUT + KD
G_PEER = G_XT + 2 * TT
G_YT = G_PEER + 5 * PEER_HEADS

CONST = {}
for _name, _n in (("ident", P), ("rot", P), ("cos", S), ("sin", S), ("inv_cnt", 4 * S),
                  ("iota", TOPK), ("tri", S), ("mask", P), ("inv_freq", 1)):
    CONST[_name] = (sum(n for _, n in CONST.values()), _n)
NCONST = sum(n for _, n in CONST.values())

D_FF = 2816
KF = D_FF // P
SSD_INNER, SSD_HEADS, SSD_HEAD_DIM, SSD_GROUPS, CONV = 2048, 32, 64, 4, 4
KX = SSD_INNER // P
HPG = SSD_HEADS // SSD_GROUPS
MLA_HEADS, MLA_NOPE, MLA_ROPE = 8, 128, 64
MLA_QK = MLA_NOPE + MLA_ROPE
PAIRS = MLA_HEADS // 2
Q_LORA, KV_LORA = 512, 256
KQ, KC = Q_LORA // P, KV_LORA // P
TILES_2 = (2 * 3 * KF * KD + (1 + 2 * SSD_GROUPS + 2 * KX + KQ + KC + 1 + 2 * KD) * KD
           + (MLA_HEADS + PAIRS) * KQ + 2 * MLA_HEADS * KC + KX * KD + 2 * KD * KD)
CHUNKS_2 = -(-TILES_2 // TILES)

PAR_2 = {}
for _name, _n in (("ln_ffn1", KD), ("ln_mix", KD), ("ln_ffn2", KD), ("conv_w", CONV * 24), ("conv_b", 24),
                  ("d_skip", KX), ("ssd_norm", KX), ("q_lora", KQ), ("kv_lora", KC), ("q_nope", 1),
                  ("q_rope", 1), ("k_nope", 1), ("k_rope", 1), ("a_log", SSD_HEADS),
                  ("dt_bias", SSD_HEADS)):
    PAR_2[_name] = (sum(n for _, n in PAR_2.values()), _n)
NPAR_2 = sum(n for _, n in PAR_2.values())

H_FFN1 = 0
H_FFN1_OUT = H_FFN1 + 2 * KF
H_DT = H_FFN1_OUT + KD


def columns(tile, table, name):
    at, n = table[name]
    return tile[:, at:at + n]


def evacuated(eng, g_free, g):
    eng.wait_ge(g_free[g % GB], g // GB + 1)


def bank_free(pe, g_free, g):
    if g >= GB:
        evacuated(pe, g_free, g - GB)


class WeightStream:

    def __init__(self, pe, ring, loaded, used):
        self.pe, self.ring, self.loaded, self.used = pe, ring, loaded, used
        self.slots = len(loaded)
        self.at = self.done = 0

    def take(self, n):
        tiles = []
        for _ in range(n):
            chunk, r = divmod(self.at, TILES)
            if r == 0:
                self.pe.wait_ge(self.loaded[chunk % self.slots], 16 * (chunk // self.slots + 1))
            tiles.append(self.ring[:, chunk % self.slots, r * P:(r + 1) * P])
            self.at += 1
        return tiles

    def free(self, mm, before):
        n = before // TILES - self.done
        if n > 0:
            mm.then_inc(self.used, n)
            self.done += n


def load_weights(sp, stream, layer, chunks, ring, loaded, used):
    first, slots = layer * chunks, len(loaded)
    turns = chunks // slots

    def load(chunk, c):
        sp.dma_start(ring[:, c, :], stream[bass.ds(first + chunk, 1), :, :].rearrange("o p n -> p (o n)")
                     ).then_inc(loaded[c], 16)

    for c in range(slots):
        load(c, c)
    with sp.Fori(1, turns) as turn:
        for c in range(slots):
            sp.wait_ge(used, (turn - 1) * slots + (c + 1))
            load(turn * slots + c, c)
    for c in range(turns * slots, chunks):
        sp.wait_ge(used, c - slots + 1)
        load(c, c % slots)


def first_layer(nc, layer, T, sem):
    x, const, ring = T["x"], T["const"], T["ring"]
    par, mod, scale1 = T["par"], T["mod"], T["scale1"]
    sq, xn, xm, std, rstd = T["sq"], T["xn"], T["xm"], T["std"], T["rstd"]
    G, M = T["G"], T["M"]
    NORM, SC, PT, OB = M[:, 0, :], M[:, 1, :], M[:, 2, :], M[:, 3, :]
    qsq, qw, rope1, rope2, qk = T["qsq"], T["qw"], T["rope1"], T["rope2"], T["qk"]
    v_tok, probs, probsT, attn = T["v_tok"], T["probs"], T["probsT"], T["attn"]
    smax, nbias, rsum, rinv = T["smax"], T["nbias"], T["rsum"], T["rinv"]
    gates, upad, win, pooled, mixed, merged = (T["gates"], T["upad"], T["win"], T["pooled"],
                                               T["mixed"], T["merged"])
    ident = columns(const, CONST, "ident")
    rot = columns(const, CONST, "rot")
    cos, sin = columns(const, CONST, "cos"), columns(const, CONST, "sin")
    inv_cnt = columns(const, CONST, "inv_cnt").rearrange("p (g t) -> p g t", g=4)
    iota = columns(const, CONST, "iota")
    g_free, g_full = sem["g_free"], sem["g_full"]
    att_scale = float(HEAD_DIM) ** -0.5
    q_at = {4 + h: h for h in range(HEADS)}
    unit_at = {0: 0, 1: 1} | {4 + h: KV_HEADS + h for h in range(HEADS)}
    U0, GA0 = 2 * KV_HEADS + HEADS, 2 * KV_HEADS + HEADS + 4
    POOL_STEP = 20

    def ada(part):
        return mod[:, part * KD:(part + 1) * KD]

    def halves(tile):
        return tile.rearrange("p (a t) -> p a t", a=2)

    block = nc.Block()
    with block:
        @block.sync
        def _(sp):
            sp.dma_start(par[:, 0:NPAR_1], T["par1"][bass.ds(layer, 1), :, :].rearrange(
                "o p n -> p (o n)")).then_inc(sem["par_loaded"], 16)
            load_weights(sp, T["stream1"], layer, CHUNKS_1, ring, sem["w_loaded"], sem["w_used"])

        @block.gpsimd
        def _(pool):
            def gather(table, buf, landed, used, r, k):
                n = r * TOPK + k
                if n >= SLOTS:
                    pool.wait_ge(used, n - SLOTS + 1)
                pool.indirect_dma_start(
                    buf[:, n % SLOTS, :], None, table,
                    bass.IndirectOffsetOnAxis(ap=T["expert"][:, r, k:k + 1], axis=0)
                ).then_inc(landed[n % SLOTS], 16)

            for r in range(ROUNDS + 1):
                if r < ROUNDS:
                    pool.wait_ge(sem["routed"], r + 1)
                for k in range(TOPK):
                    if r < ROUNDS:
                        gather(T["expert_u"], T["u_rows"], sem["u_landed"], sem["u_used"], r, k)
                    if r >= 1:
                        gather(T["expert_v"], T["v_rows"], sem["v_landed"], sem["v_used"], r - 1, k)
            for n in range(SLOTS):
                pool.wait_ge(sem["u_landed"][n], 16 * (ROUNDS * TOPK // SLOTS))
                pool.wait_ge(sem["v_landed"][n], 16 * (ROUNDS * TOPK // SLOTS))

        @block.tensor
        def _(pe):
            w = WeightStream(pe, ring, sem["w_loaded"], sem["w_used"])

            def ada_chunks(col, n, done):
                for j in range(col, col + n):
                    before = w.at
                    tiles = w.take(KD)
                    for k in range(KD):
                        mm = pe.matmul(OB[:, S + j:S + j + 1], tiles[k], T["c_act"][:, k:k + 1],
                                       start=(k == 0), stop=(k == KD - 1))
                        if k == 0:
                            w.free(mm, before)
                if done:
                    mm.then_inc(sem["ada_full"], 1)

            def project(g, rhs, kt, ready=None):
                bank_free(pe, g_free, g)
                before = w.at
                tiles = w.take(kt)
                for k in range(kt):
                    if ready:
                        ready(k)
                    mm = pe.matmul(G[:, g % GB, 0:S], tiles[k], rhs(k), start=(k == 0), stop=(k == kt - 1))
                    if k == 0 and kt > 1:
                        w.free(mm, before)
                mm.then_inc(g_full, 1)

            def mean_square(n):
                for k in range(KD):
                    pe.wait_ge(sem["sq_ready"], n * KD + k + 1)
                    mm = pe.matmul(NORM[:, 0:S], T["ones_d"][:, :], sq[:, k, :], start=(k == 0),
                                   stop=(k == KD - 1))
                mm.then_inc(sem["norm_full"], 1)

            def unit(u):
                pe.wait_ge(sem["std_ready"], u + 1)
                if u >= 1:
                    pe.wait_ge(sem["rope_read"], u)
                evacuated(pe, g_free, G_IN + (u if u < KV_HEADS else u + KV_HEADS))
                pe.matmul(NORM[:, 0:S], T["ones_h"][:, :], qsq[:, u % 2, :], start=True, stop=True)
                pe.matmul(NORM[:, S:2 * S], rot, qw[:, u % 2, :], start=True, stop=True
                          ).then_inc(sem["norm_full"], 1)

            def scores(h):
                pe.wait_ge(sem["qk_ready"], KV_HEADS + h + 1)
                if h >= 1:
                    pe.wait_ge(sem["exp_done"], TT * h)
                for t in range(TT):
                    mm = pe.matmul(SC[:, t * S:(t + 1) * S], qk[:, KV_HEADS + h, t * P:(t + 1) * P],
                                   qk[:, h // GROUP, :], start=True, stop=True)
                mm.then_inc(sem["s_full"], 1)

            def turn_probs(h):
                pe.wait_ge(sem["p_ready"], h + 1)
                if h >= 1:
                    pe.wait_ge(sem["pt_ready"], h)
                for kt in range(TT):
                    for t in range(TT):
                        mm = pe.transpose(PT[:, kt * S + t * P:kt * S + (t + 1) * P],
                                          probs[:, h % 2, t, kt * P:(kt + 1) * P], ident)
                mm.then_inc(sem["pt_full"], 1)

            def values(h):
                pe.wait_ge(sem["pt_ready"], h + 1)
                if h >= 1:
                    pe.wait_ge(sem["o_ready"], h)
                if h == 0:
                    for g in range(KV_HEADS):
                        evacuated(pe, g_free, G_IN + KV_HEADS + g)
                for kt in range(TT):
                    mm = pe.matmul(OB[:, 0:S], v_tok[:, kt, h // GROUP, :], probsT[:, h % 2, kt, :],
                                   start=(kt == 0), stop=(kt == TT - 1))
                mm.then_inc(sem["o_full"], 1)

            ada_chunks(0, 2 * KD, True)
            mean_square(0)

            def xm_ready(k):
                pe.wait_ge(sem["xm_ready"], k + 1)

            for i in range(T_IN):
                if KV_HEADS <= i < 2 * KV_HEADS:
                    bank_free(pe, g_free, i)
                    before = w.at
                    tiles = w.take(KD)
                    for t in range(TT):
                        for k in range(KD):
                            mm = pe.matmul(G[:, i % GB, t * P:(t + 1) * P], xm[:, k, t * P:(t + 1) * P],
                                           tiles[k], start=(k == 0), stop=(k == KD - 1))
                            if k == 0 and t == 0:
                                w.free(mm, before)
                    mm.then_inc(g_full, 1)
                else:
                    project(G_IN + i, lambda k: xm[:, k, :], KD, xm_ready if i == 0 else None)
                n = sum(j < i - 7 for j in q_at)
                if n:
                    pe.wait_ge(sem["o_ready"], n)
                ada_chunks(2 * KD + i, 1, i == T_IN - 1)
                if i - 1 in unit_at:
                    unit(unit_at[i - 1])
                if i - 3 in q_at:
                    scores(q_at[i - 3])
                if i - 5 in q_at:
                    turn_probs(q_at[i - 5])
                if i - 7 in q_at:
                    values(q_at[i - 7])

            for g in range(4):
                pe.wait_ge(sem["pooled"], g + 1)
                project(G_MIX + g, lambda k: pooled[:, g, :], 1)
            for g in range(4):
                evacuated(pe, g_free, G_MIX + g)
            for j in range(KD):
                project(G_POOLO + j, lambda k: mixed[:, k, :], 4)
            pe.wait_ge(sem["o_ready"], HEADS)
            for j in range(KD):
                project(G_ATTO + j, lambda k: attn[:, k, :], KD)
            pe.wait_ge(sem["merged"], KD)
            for j in range(KD):
                project(G_OUT + j, lambda k: merged[:, k, :], KD)

            mean_square(1)
            pe.wait_ge(sem["xm_ready"], 2 * KD)
            for t in range(TT):
                for half in range(2):
                    g = G_XT + 2 * t + half
                    bank_free(pe, g_free, g)
                    for q in range(4):
                        mm = pe.transpose(G[:, g % GB, q * P:(q + 1) * P],
                                          xm[:, 4 * half + q, t * P:(t + 1) * P], ident)
                    mm.then_inc(g_full, 1)

            def queries(h):
                g = G_PEER + 5 * h
                for j in range(4):
                    project(g + j, lambda k: xm[:, k, :], KD)
                for j in range(4):
                    evacuated(pe, g_free, g + j)
                before = w.at
                tiles = w.take(4)
                for t in range(TT):
                    for p in range(2):
                        for k in range(2):
                            at = (2 * t + p) * P
                            mm = pe.matmul(G[:, (g + 4) % GB, at:at + P],
                                           T["query"][:, h % 2, 2 * p + k, t * P:(t + 1) * P],
                                           tiles[2 * p + k], start=(k == 0), stop=(k == 1))
                            if t == p == k == 0:
                                w.free(mm, before)
                mm.then_inc(g_full, 1)

            def add_experts(r):
                h, t = divmod(r, TT)
                for k in range(TOPK):
                    n = r * TOPK + k
                    pe.wait_ge(sem["v_landed"][n % SLOTS], 16 * (n // SLOTS + 1))
                    pe.wait_ge(sem["diag_ready"], n + 1)
                    for half in range(2):
                        mm = pe.matmul(M[:, 2 * t + half, :], T["diag"][:, n % 4, :],
                                       T["v_rows"][:, n % SLOTS, half * 512:(half + 1) * 512],
                                       start=(h == 0 and k == 0), stop=(h == PEER_HEADS - 1 and k == TOPK - 1))
                    mm.then_inc(sem["v_used"], 1)

            queries(0)
            queries(1)
            pe.wait_ge(sem["std_ready"], UNITS + 2)
            for h in range(PEER_HEADS):
                for t in range(TT):
                    add_experts(h * TT + t)
                if h + 2 < PEER_HEADS:
                    queries(h + 2)
            for t in range(TT):
                pe.wait_ge(sem["y_copied"], t + 1)
                for half in range(2):
                    g = G_YT + 2 * t + half
                    bank_free(pe, g_free, g)
                    for q in range(4):
                        mm = pe.transpose(G[:, g % GB, q * P:(q + 1) * P],
                                          T["y_tok"][:, t, (4 * half + q) * P:(4 * half + q + 1) * P], ident)
                    mm.then_inc(g_full, 1)

        @block.scalar
        def _(act):
            def copy_out(g, out, width=S, func=ACT.Copy, **kw):
                act.wait_ge(g_full, g + 1)
                act.activation(out, G[:, g % GB, 0:width], func, **kw).then_inc(g_free[g % GB], 1)

            def squares(n, ready=None):
                for k in range(KD):
                    if ready:
                        ready(k)
                    act.activation(sq[:, k, :], x[:, k, :], ACT.Square).then_inc(sem["sq_ready"], 1)

            def root(n):
                act.wait_ge(sem["norm_full"], n + 1)
                if n >= 1:
                    act.wait_ge(sem["rstd_ready"], n)
                act.activation(std[:, :], NORM[:, 0:S], ACT.Sqrt, bias=T["eps"][:, :]
                               ).then_inc(sem["std_ready"], 1)

            def modulate(n, shift):
                for k in range(KD):
                    act.wait_ge(sem["xn_ready"], n * KD + k + 1)
                    act.activation(xm[:, k, :], xn[:, k, :], ACT.Identity, bias=ada(shift)[:, k:k + 1],
                                   scale=scale1[:, n, k:k + 1]).then_inc(sem["xm_ready"], 1)

            def exps(h):
                act.wait_ge(sem["bias_ready"], h + 1)
                if h >= 2:
                    act.wait_ge(sem["pt_full"], h - 1)
                for t in range(TT):
                    act.activation(probs[:, h % 2, t, :], SC[:, t * S:(t + 1) * S], ACT.Exp,
                                   bias=nbias[:, h, t:t + 1], scale=att_scale,
                                   accum_out=rsum[:, h, t:t + 1]).then_inc(sem["exp_done"], 1)

            squares(0)
            root(0)
            modulate(0, 0)
            act.wait_ge(sem["par_loaded"], 16)
            for i in range(T_IN):
                g = G_IN + i
                if i in unit_at:
                    u = unit_at[i]
                    if u >= 2:
                        act.wait_ge(sem["qk_ready"], u - 1)
                        act.wait_ge(sem["norm_full"], u)
                    act.wait_ge(g_full, g + 1)
                    act.activation(qsq[:, u % 2, :], G[:, g % GB, 0:S], ACT.Square)
                    copy_out(g, qw[:, u % 2, :], scale=columns(par, PAR_1, "k_norm" if u < KV_HEADS
                                                              else "q_norm"))
                elif i < 2 * KV_HEADS:
                    copy_out(g, v_tok[:, :, i - KV_HEADS, :])
                elif i < GA0:
                    if i == U0:
                        act.wait_ge(sem["pads_ready"], 2)
                    copy_out(g, upad[:, i - U0, PADW:PADW + S])
                else:
                    copy_out(g, gates[:, i - GA0, :], func=ACT.Sigmoid)
                if i - 1 in unit_at:
                    root(1 + unit_at[i - 1])
                if i - 3 in q_at:
                    exps(q_at[i - 3])
                if i - 5 in q_at:
                    h = q_at[i - 5]
                    act.wait_ge(sem["pt_full"], h + 1)
                    if h >= 2:
                        act.wait_ge(sem["o_full"], h - 1)
                    act.activation(probsT[:, h % 2, :, :], halves(PT), ACT.Copy).then_inc(sem["pt_ready"], 1)
                if i - 7 in q_at:
                    h = q_at[i - 7]
                    act.wait_ge(sem["o_full"], h + 1)
                    act.activation(attn[:, h, :], OB[:, 0:S], ACT.Copy).then_inc(sem["o_ready"], 1)
            for g in range(4):
                copy_out(G_MIX + g, mixed[:, g, :], scale=columns(par, PAR_1, "pool_scale")[:, g:g + 1])
            squares(1, lambda k: evacuated(act, g_free, G_OUT + k))
            root(UNITS + 1)
            modulate(1, 3)
            for t in range(TT):
                for half in range(2):
                    copy_out(G_XT + 2 * t + half, T["x_tok"][:, t, half * 512:(half + 1) * 512], 512)

            def queries(h):
                g = G_PEER + 5 * h
                for j in range(4):
                    copy_out(g + j, T["query"][:, h % 2, j, :])
                copy_out(g + 4, T["key_score"][:, h, :], 4 * P)

            def expert_softmax(r):
                act.wait_ge(sem["top_ready"], r + 1)
                act.activation(T["gate"][:, r, :], T["top"][:, r, :], ACT.Exp, bias=T["neg_top"][:, r:r + 1],
                               accum_out=T["gate_sum"][:, r:r + 1]).then_inc(sem["gate_exp"], 1)

            def diagonals(r):
                act.wait_ge(sem["u_used"], TOPK * (r + 1))
                act.activation(T["gelu"][:, r, :], T["hid"][:, r, :], ACT.Gelu).then_inc(sem["gelu_done"], 1)
                act.wait_ge(sem["weight_ready"], r + 1)
                for k in range(TOPK):
                    n = r * TOPK + k
                    if n >= 4:
                        act.wait_ge(sem["v_used"], n - 3)
                    act.activation(T["diag"][:, n % 4, :], ident, ACT.Copy, scale=T["weight"][:, r, k:k + 1]
                                   ).then_inc(sem["diag_ready"], 1)

            queries(0)
            queries(1)
            expert_softmax(0)
            expert_softmax(1)
            for r in range(ROUNDS):
                diagonals(r)
                if r + 2 < ROUNDS:
                    expert_softmax(r + 2)
                if r % TT == TT - 1 and r // TT + 2 < PEER_HEADS:
                    queries(r // TT + 2)
            act.wait_ge(sem["v_used"], ROUNDS * TOPK)
            for t in range(TT):
                act.activation(T["y_tok"][:, t, :], M[:, 2 * t:2 * t + 2, :].rearrange("p a n -> p (a n)"),
                               ACT.Copy).then_inc(sem["y_copied"], 1)

        @block.vector
        def _(dve):
            chain = [0]

            def link(ins):
                chain[0] += 1
                ins.then_inc(sem["dve_chain"], 1)
                dve.wait_ge(sem["dve_chain"], chain[0])

            def ada_bias(at, n, done):
                dve.wait_ge(sem["ada_full"], done)
                link(dve.tensor_tensor(mod[:, at:at + n], OB[:, S + at:S + at + n],
                                       columns(par, PAR_1, "ada_b")[:, at:at + n], ALU.add))

            def scale_of(n, part, name):
                link(dve.scalar_tensor_tensor(out=scale1[:, n, :], in0=ada(part), scalar=1.0,
                                              in1=columns(par, PAR_1, name), op0=ALU.add, op1=ALU.mult))

            def inverse_std(n):
                dve.wait_ge(sem["std_ready"], n + 1)
                dve.reciprocal(rstd[:, :], std[:, :]).then_inc(sem["rstd_ready"], 1)
                dve.wait_ge(sem["rstd_ready"], n + 1)

            def normalise(n):
                for k in range(KD):
                    dve.tensor_tensor(xn[:, k, :], x[:, k, :], rstd[:, :], ALU.mult
                                      ).then_inc(sem["xn_ready"], 1)

            def unit(u):
                inverse_std(u + 1)
                link(dve.tensor_tensor(rope1[:, :], qw[:, u % 2, :], cos, ALU.mult))
                dve.tensor_tensor(rope2[:, :], NORM[:, S:2 * S], sin, ALU.mult).then_inc(sem["rope_read"], 1)
                dve.wait_ge(sem["rope_read"], u + 1)
                link(dve.tensor_tensor(rope1[:, :], rope1[:, :], rope2[:, :], ALU.add))
                dve.tensor_tensor(qk[:, u, :], rope1[:, :], rstd[:, :], ALU.mult).then_inc(sem["qk_ready"], 1)
                dve.wait_ge(sem["qk_ready"], u + 1)

            def softmax(h):
                dve.wait_ge(sem["s_full"], h + 1)
                link(dve.tensor_reduce(smax[:, h, :], halves(SC), AX_X, ALU.max))
                dve.tensor_scalar(nbias[:, h, :], smax[:, h, :], -att_scale, None, ALU.mult
                                  ).then_inc(sem["bias_ready"], 1)
                dve.wait_ge(sem["exp_done"], TT * (h + 1))
                link(dve.reciprocal(rinv[:, h, :], rsum[:, h, :]))
                dve.tensor_tensor(probs[:, h % 2, :, :], probs[:, h % 2, :, :],
                                  rinv[:, h, :].unsqueeze(2).to_broadcast([P, TT, S]), ALU.mult
                                  ).then_inc(sem["p_ready"], 1)

            def pool_group(g):
                evacuated(dve, g_free, G_IN + U0 + g)
                src, at, lo, hi = upad[:, g, :], 0, 0, S + 2 * PADW
                half, width = 1, 2
                a, b = PADW - 7, PADW + S + 7
                link(dve.tensor_tensor(win[:, 0, a:b], src[:, a - 1:b - 1], src[:, a:b], ALU.add))
                cur = 0
                while width < POOL_WINDOWS[g]:
                    a, b = a + half, b - half
                    link(dve.tensor_tensor(win[:, 1 - cur, a:b], win[:, cur, a - half:b - half],
                                           win[:, cur, a + half:b + half], ALU.add))
                    cur, width, half = 1 - cur, 2 * width, 2 * half
                link(dve.tensor_tensor(win[:, cur, PADW:PADW + S], win[:, cur, PADW:PADW + S],
                                       inv_cnt[:, g, :], ALU.mult))
                dve.tensor_tensor(pooled[:, g, :], win[:, cur, PADW:PADW + S], src[:, PADW:PADW + S],
                                  ALU.subtract).then_inc(sem["pooled"], 1)
                dve.wait_ge(sem["pooled"], g + 1)

            dve.memset(upad[:, :, 0:PADW], 0.0).then_inc(sem["pads_ready"], 1)
            dve.memset(upad[:, :, PADW + S:], 0.0).then_inc(sem["pads_ready"], 1)
            dve.wait_ge(sem["pads_ready"], 2)
            dve.wait_ge(sem["par_loaded"], 16)
            ada_bias(0, 2 * KD, 1)
            scale_of(0, 1, "norm_mix")
            inverse_std(0)
            normalise(0)
            for i in range(T_IN):
                if i - 1 in unit_at:
                    unit(unit_at[i - 1])
                if i - 3 in q_at:
                    softmax(q_at[i - 3])
                if POOL_STEP <= i < POOL_STEP + 4:
                    pool_group(i - POOL_STEP)
            ada_bias(2 * KD, 4 * KD, 2)
            scale_of(1, 4, "norm_ffn")
            for j in range(KD):
                g = G_POOLO + j
                evacuated(dve, g_free, G_IN + GA0 + KD + j)
                dve.wait_ge(g_full, g + 1)
                dve.tensor_tensor(merged[:, j, :], G[:, g % GB, 0:S], gates[:, KD + j, :], ALU.mult
                                  ).then_inc(g_free[g % GB], 1)
            for j in range(KD):
                g = G_ATTO + j
                dve.wait_ge(g_full, g + 1)
                dve.tensor_tensor(gates[:, j, :], G[:, g % GB, 0:S], gates[:, j, :], ALU.mult
                                  ).then_inc(g_free[g % GB], 1)
                evacuated(dve, g_free, g)
                dve.tensor_tensor(merged[:, j, :], merged[:, j, :], gates[:, j, :], ALU.add
                                  ).then_inc(sem["merged"], 1)
            for j in range(KD):
                g = G_OUT + j
                dve.wait_ge(g_full, g + 1)
                dve.scalar_tensor_tensor(out=x[:, j, :], in0=G[:, g % GB, 0:S], scalar=ada(2)[:, j:j + 1],
                                         in1=x[:, j, :], op0=ALU.mult, op1=ALU.add
                                         ).then_inc(g_free[g % GB], 1)
            inverse_std(UNITS + 1)
            normalise(1)

            def route(r):
                h, t = divmod(r, TT)
                evacuated(dve, g_free, G_PEER + 5 * h + 4)
                val, idx, idxf, rest = T["val"], T["idx"], T["idxf"], T["rest"]
                for p in range(2):
                    s = T["key_score"][:, h, (2 * t + p) * P:(2 * t + p + 1) * P]
                    link(dve.max(out=val[:, p, 0:8], in_=s))
                    dve.max_index(out=idx[:, p, 0:8], in_max=val[:, p, 0:8], in_values=s)
                    link(dve.match_replace(out=rest[:, 0:N_KEYS], in_to_replace=val[:, p, 0:8],
                                           in_values=s, imm_value=NEG))
                    link(dve.max(out=val[:, p, 8:16], in_=rest[:, 0:N_KEYS]))
                    link(dve.max_index(out=idx[:, p, 8:16], in_max=val[:, p, 8:16],
                                       in_values=rest[:, 0:N_KEYS]))
                link(dve.tensor_copy(idxf[:, :, :], idx[:, :, :]))
                cand = T["cand"]
                link(dve.tensor_tensor(cand[:, :].rearrange("p (i j) -> p i j", i=TOPK),
                                       val[:, 0, :].unsqueeze(2).to_broadcast([P, TOPK, TOPK]),
                                       val[:, 1, :].unsqueeze(1).to_broadcast([P, TOPK, TOPK]), ALU.add))
                top, pos = T["top"][:, r, :], T["pos"]
                link(dve.max(out=top[:, 0:8], in_=cand[:, :]))
                dve.max_index(out=pos[:, 0:8], in_max=top[:, 0:8], in_values=cand[:, :])
                link(dve.match_replace(out=rest[:, :], in_to_replace=top[:, 0:8], in_values=cand[:, :],
                                       imm_value=NEG))
                link(dve.max(out=top[:, 8:16], in_=rest[:, :]))
                link(dve.max_index(out=pos[:, 8:16], in_max=top[:, 8:16], in_values=rest[:, :]))
                dve.tensor_scalar(T["neg_top"][:, r:r + 1], top[:, 0:1], -1.0, None, ALU.mult
                                  ).then_inc(sem["top_ready"], 1)
                link(dve.tensor_scalar(T["pos_ij"][:, 0, :], pos[:, :], 4, None, ALU.logical_shift_right))
                link(dve.tensor_scalar(T["pos_ij"][:, 1, :], pos[:, :], 15, None, ALU.bitwise_and))
                link(dve.tensor_copy(T["pos_f"][:, :, :], T["pos_ij"][:, :, :]))
                pick, key = T["pick"], T["key"]
                for p in range(2):
                    link(dve.tensor_tensor(pick[:, :, :],
                                           T["pos_f"][:, p, :].unsqueeze(2).to_broadcast([P, TOPK, TOPK]),
                                           iota.unsqueeze(1).to_broadcast([P, TOPK, TOPK]), ALU.is_equal))
                    link(dve.tensor_tensor(pick[:, :, :], pick[:, :, :],
                                           idxf[:, p, :].unsqueeze(1).to_broadcast([P, TOPK, TOPK]), ALU.mult))
                    link(dve.tensor_reduce(key[:, p, :], pick[:, :, :], AX_X, ALU.add))
                link(dve.scalar_tensor_tensor(out=key[:, 0, :], in0=key[:, 0, :], scalar=float(N_KEYS),
                                              in1=key[:, 1, :], op0=ALU.mult, op1=ALU.add))
                dve.tensor_scalar(T["expert"][:, r, :], key[:, 0, :], T["first_expert"][:, :], None, ALU.add
                                  ).then_inc(sem["routed"], 1)

            def gate_norm(r):
                dve.wait_ge(sem["gate_exp"], r + 1)
                link(dve.reciprocal(T["gate_inv"][:, r:r + 1], T["gate_sum"][:, r:r + 1]))

            def products(r):
                t = r % TT
                if r == 0:
                    for g in range(2 * TT):
                        evacuated(dve, g_free, G_XT + g)
                for k in range(TOPK):
                    n = r * TOPK + k
                    row = T["u_rows"][:, n % SLOTS, :]
                    dve.wait_ge(sem["u_landed"][n % SLOTS], 16 * (n // SLOTS + 1))
                    dve.tensor_tensor_reduce(row, row, T["x_tok"][:, t, :], 1.0, 0.0, ALU.mult, ALU.add,
                                             T["hid"][:, r, k:k + 1]).then_inc(sem["u_used"], 1)
                gate_norm(r)
                dve.wait_ge(sem["gelu_done"], r + 1)
                dve.scalar_tensor_tensor(out=T["weight"][:, r, :], in0=T["gelu"][:, r, :],
                                         scalar=T["gate_inv"][:, r:r + 1], in1=T["gate"][:, r, :],
                                         op0=ALU.mult, op1=ALU.mult).then_inc(sem["weight_ready"], 1)

            route(0)
            route(1)
            for r in range(ROUNDS):
                products(r)
                if r + 2 < ROUNDS:
                    route(r + 2)
            link(dve.tensor_scalar(T["first_expert"][:, :], T["first_expert"][:, :], float(N_EXPERTS), None,
                                   ALU.add))
            for t in range(TT):
                for half in range(2):
                    g = G_YT + 2 * t + half
                    dve.wait_ge(g_full, g + 1)
                    for q in range(4):
                        k = 4 * half + q
                        ins = dve.scalar_tensor_tensor(out=x[:, k, t * P:(t + 1) * P],
                                                       in0=G[:, g % GB, q * P:(q + 1) * P],
                                                       scalar=ada(5)[:, k:k + 1], in1=x[:, k, t * P:(t + 1) * P],
                                                       op0=ALU.mult, op1=ALU.add)
                    ins.then_inc(g_free[g % GB], 1)


MIX_STEPS = ([("dt", 0)] + [("bc", j) for j in range(2 * SSD_GROUPS)] + [("xs", j) for j in range(KX)]
             + [("z", j) for j in range(KX)] + [("cq", j) for j in range(KQ)]
             + [("ckv", j) for j in range(KC)] + [("kr", 0)] + [("q_rope", j) for j in range(PAIRS)]
             + [s for j in range(2 * KD) for s in (("gate", j), ("nope", j))]
             + [("v", j) for j in range(MLA_HEADS)] + [("ssd_out", j) for j in range(KD)]
             + [("mla_out", j) for j in range(KD)] + [("out", j) for j in range(KD)])
STEP_OF = {s: i for i, s in enumerate(MIX_STEPS)}
SIDE = {}


def _side(step, what, n):
    SIDE.setdefault(step, []).append((what, n))


_side(STEP_OF["dt", 0] + 2, "acum", 0)
for _j in range(2 * SSD_GROUPS):
    _side(STEP_OF["bc", _j], "conv", _j)
    _side(STEP_OF["bc", _j] + 1, "conv_act", _j)
for _j in range(KX):
    _side(STEP_OF["xs", _j], "conv", 2 * SSD_GROUPS + _j)
    _side(STEP_OF["xs", _j] + 1, "conv_act", 2 * SSD_GROUPS + _j)
    _side(STEP_OF["xs", _j] + 3, "turn_x", _j)
    _side(STEP_OF["z", _j] + 2, "decay", 2 * _j)
    _side(STEP_OF["z", _j] + 2, "decay", 2 * _j + 1)
    _side(STEP_OF["z", _j] + 3, "scan", _j)
for _g in range(SSD_GROUPS):
    _side(STEP_OF["xs", 2 + _g], "cb", _g)
_side(STEP_OF["ckv", 0], "norm_cq", 0)
_side(STEP_OF["kr", 0], "norm_ckv", 0)
_side(STEP_OF["kr", 0] + 1, "rotate", PAIRS)
for _j in range(PAIRS):
    _side(STEP_OF["q_rope", _j] + 1, "rotate", _j)
_side(STEP_OF["q_rope", 3], "norm_ssd", 0)
for _j in range(2 * MLA_HEADS):
    _side(STEP_OF["nope", _j] + 1, "unit", _j)
for _j in range(MLA_HEADS):
    _side(STEP_OF["ssd_out", _j], "softmax", _j)
    _side(STEP_OF["ssd_out", _j] + 1, "turn_probs", _j)
    _side(STEP_OF["ssd_out", _j] + 2, "values", _j)
SIDE[STEP_OF["mla_out", 1]].remove(("values", 7))
SIDE[STEP_OF["mla_out", 0]].remove(("turn_probs", 7))
SIDE[STEP_OF["mla_out", 0]].remove(("values", 6))
SIDE[STEP_OF["ssd_out", 7]] += [("values", 6), ("turn_probs", 7), ("values", 7)]

TURN, TURN_X = {}, {}
_g = H_DT
for _i, _s in enumerate(MIX_STEPS):
    TURN[_s] = _g
    _g += 1
    for _what, _n in SIDE.get(_i, []):
        if _what == "turn_x":
            TURN_X[_n] = _g
            _g += 1
H_FFN2 = _g
H_FFN2_OUT = H_FFN2 + 2 * KF
H_END = H_FFN2_OUT + KD

_order = [(KD, True)] * (2 * KF) + [(KF, True)] * KD
_turns = list(range(H_FFN1, H_DT))
for _s in MIX_STEPS:
    _kt = {"q_rope": KQ, "v": KC, "ssd_out": KX}.get(_s[0], KD)
    if _s[0] == "nope":
        _kt = KQ if _s[1] < MLA_HEADS else KC
    _order.append((_kt, _s[0] in ("bc", "xs", "z", "cq", "ckv", "kr", "gate")))
    _turns.append(TURN[_s])
_order += [(KD, True)] * (2 * KF) + [(KF, True)] * KD
_turns += list(range(H_FFN2, H_END))
HALVED = [False] * CHUNKS_2
LAST_CHUNK = {}
_at = 0
for (_kt, _halved), _g in zip(_order, _turns):
    for _t in range(_at, _at + _kt):
        HALVED[_t // TILES] |= _halved
    _at += _kt
    LAST_CHUNK[_g] = (_at - 1) // TILES
assert _at == TILES_2
HALVED_CHUNKS = [c for c in range(CHUNKS_2) if HALVED[c]]
HALVED_AT = {c: n for n, c in enumerate(HALVED_CHUNKS)}


class Halves:

    def __init__(self, eng, cut):
        self.eng, self.cut, self.n = eng, cut, 0

    def ahead(self, g):
        while self.n < len(HALVED_CHUNKS) and HALVED_CHUNKS[self.n] <= LAST_CHUNK[g] + PARTS - 1:
            self.cut(self.n, HALVED_CHUNKS[self.n])
            self.n += 1


NORM_OF = {"ffn1": 0, "mix": 1, "cq": 2, "ckv": 3, "ssd": 4, "unit": 5, "ffn2": 5 + 2 * MLA_HEADS}


def second_layer(nc, layer, T, sem):
    x, const, ring, par = T["x"], T["const"], T["ring"], T["par"]
    xm, std, rstd, G, M = T["xm"], T["std"], T["rstd"], T["G"], T["M"]
    NORM, SC, PT, OB = M[:, 0, :], M[:, 1, :], M[:, 2, :], M[:, 3, :]
    ident, tri, mask, rot = (columns(const, CONST, n) for n in ("ident", "tri", "mask", "rot"))
    g_free, g_full = sem["g_free"], sem["g_full"]
    ff_high, ff_low, silu, ff = T["ff_high"], T["ff_low"], T["silu"], T["ff"]
    w_loaded = sem["w_loaded"][:RING_2]
    qk_scale = float(MLA_QK) ** -0.5

    def p2(name):
        return columns(par, PAR_2, name)

    def halves(tile):
        return tile.rearrange("p (a t) -> p a t", a=2)

    def gn(s):
        return TURN[s]

    block = nc.Block()
    with block:
        @block.sync
        def _(sp):
            sp.dma_start(par[:, 0:NPAR_2], T["par2"][bass.ds(layer, 1), :, :].rearrange(
                "o p n -> p (o n)")).then_inc(sem["par_loaded"], 16)
            load_weights(sp, T["stream2"], layer, CHUNKS_2, ring, w_loaded, sem["w_used"])

        @block.tensor
        def _(pe):
            w = WeightStream(pe, ring, w_loaded, sem["w_used"])

            def project(g, rhs, kt, ready=None):
                bank_free(pe, g_free, g)
                for k in range(kt):
                    before = w.at
                    tile, = w.take(1)
                    mm = pe.matmul(G[:, g % GB, 0:S], tile, rhs(k), start=(k == 0), stop=(k == kt - 1))
                    if k < kt - 1:
                        w.free(mm, before)
                mm.then_inc(g_full, 1)

            def project_halved(g, high, low, kt, ready=None):
                bank_free(pe, g_free, g)
                out = G[:, g % GB, 0:S]
                for k in range(kt):
                    before = w.at
                    w.take(1)
                    chunk, r = divmod(before, TILES)
                    n = HALVED_AT[chunk]
                    if r == 0 or k == 0:
                        pe.wait_ge(sem["low_ready"], n + 1)
                    tile = slice(r * P, (r + 1) * P)
                    if ready:
                        ready(k)
                    mm = pe.matmul(out, T["w_high"][:, n % PARTS, tile], high[:, k, :], start=(k == 0), stop=False)
                    w.free(mm, before)
                    pe.matmul(out, T["w_high"][:, n % PARTS, tile], low[:, k, :], start=False, stop=False)
                    mm = pe.matmul(out, T["w_low"][:, n % PARTS, tile], high[:, k, :], start=False,
                                   stop=(k == kt - 1))
                mm.then_inc(g_full, 1)

            def project_tok(g, act, kt, width):
                bank_free(pe, g_free, g)
                before = w.at
                tiles = w.take(kt)
                for t in range(TT):
                    for k in range(kt):
                        mm = pe.matmul(G[:, g % GB, t * P:t * P + width], act(k, t), tiles[k][:, 0:width],
                                       start=(k == 0), stop=(k == kt - 1))
                        if t == k == 0:
                            w.free(mm, before)
                mm.then_inc(g_full, 1)

            def mean_square(n, count, tile, ones, ready):
                if n >= 1:
                    pe.wait_ge(sem["std_ready"], n)
                for k in range(count):
                    ready(k)
                    mm = pe.matmul(NORM[:, 0:S], ones, tile(k), start=(k == 0), stop=(k == count - 1))
                mm.then_inc(sem["norm_full"], 1)

            def norm_x(which, i):
                mean_square(NORM_OF[which], KD, lambda k: xm[:, k, :], T["ones_d"][:, :],
                            lambda k: pe.wait_ge(sem["sq_ready"], i * KD + k + 1))

            def x_halves(i):
                return lambda k: pe.wait_ge(sem["x_low_ready"], i * KD + k + 1)

            def ffn(g0, g_out, i):
                at = 0 if i == 0 else KF
                for j in range(2 * KF):
                    project_halved(g0 + j, T["x_high"], T["x_low"], KD, x_halves(i) if j == 0 else None)
                for j in range(KD):
                    project_halved(g_out + j, ff_high, ff_low, KF,
                                   (lambda k: pe.wait_ge(sem["ff_low_ready"], at + k + 1)) if j == 0 else None)

            def acum(_):
                pe.wait_ge(sem["dta_ready"], 1)
                pe.wait_ge(sem["std_ready"], 2)
                dta, U = T["dta"], tri[:, 0:P]
                n = SSD_HEADS
                pe.matmul(NORM[:, 0:n], U, dta[:, 0, :], start=True, stop=True)
                pe.matmul(NORM[:, n:2 * n], tri[:, P:S], dta[:, 0, :], start=True, stop=False)
                pe.matmul(NORM[:, n:2 * n], U, dta[:, 1, :], start=False, stop=True)
                pe.matmul(NORM[0:n, S:2 * S], dta[:, 0, :], tri, start=True, stop=False)
                pe.matmul(NORM[0:n, S + P:2 * S], dta[:, 1, :], U, start=False, stop=True
                          ).then_inc(sem["acum_full"], 1)

            def cb(g):
                pe.wait_ge(sem["conv_done"], SSD_GROUPS + g + 1)
                if g >= 1:
                    pe.wait_ge(sem["cb_ready"], g)
                b, c = T["bc"][:, g, :], T["bc"][:, SSD_GROUPS + g, :]
                pe.matmul(PT[:, 0:S], b[:, 0:P], c, start=True, stop=True)
                pe.matmul(PT[:, S:S + P], b[:, P:S], c[:, P:S], start=True, stop=True
                          ).then_inc(sem["cb_full"], 1)

            def turn_x(j):
                g = TURN_X[j]
                bank_free(pe, g_free, g)
                pe.wait_ge(sem["conv_done"], 2 * SSD_GROUPS + j + 1)
                for t in range(TT):
                    mm = pe.transpose(G[:, g % GB, t * P:(t + 1) * P], T["xs"][:, j, t * P:(t + 1) * P], ident)
                mm.then_inc(g_full, 1)

            def decay(h):
                pe.wait_ge(sem["acum_ready"], 1)
                if h == 0:
                    pe.wait_ge(sem["cb_ready"], SSD_GROUPS)
                if h >= 2:
                    pe.wait_ge(sem["seg_ready"], h - 1)
                pe.matmul((SC, PT)[h % 2][:, 0:S],
                          ident[0:SSD_HEADS, h:h + 1].to_broadcast([SSD_HEADS, P]), T["acum_h"][:, :],
                          start=True, stop=True).then_inc(sem["row_full"], 1)

            def scan(j):
                if j >= 1:
                    pe.wait_ge(sem["y_read"], j)
                evacuated(pe, g_free, TURN_X[j])
                for h in (2 * j, 2 * j + 1):
                    rows = slice(SSD_HEAD_DIM * (h % 2), SSD_HEAD_DIM * (h % 2 + 1))
                    cols = slice(h * SSD_HEAD_DIM, (h + 1) * SSD_HEAD_DIM)
                    pe.wait_ge(sem["m_ready"], h + 1)
                    pe.matmul(OB[rows, 0:S], T["xdt"][:, 0, cols], T["m"][:, h % 4, 0:S],
                              start=True, stop=False)
                    mm = pe.matmul(OB[rows, P:S], T["xdt"][:, 1, cols], T["m"][:, h % 4, S:S + P],
                                   start=False, stop=True)
                mm.then_inc(sem["y_full"], 1)

            def norm_cq(_):
                pe.wait_ge(sem["acum_ready"], 1)
                mean_square(NORM_OF["cq"], KQ, lambda k: T["lora_sq"][:, k, :], T["ones_h"][:, :],
                            lambda k: evacuated(pe, g_free, gn(("cq", k))))

            def norm_ckv(_):
                mean_square(NORM_OF["ckv"], KC, lambda k: T["lora_sq"][:, KQ + k, :], T["ones_h"][:, :],
                            lambda k: evacuated(pe, g_free, gn(("ckv", k))))

            def norm_ssd(_):
                mean_square(NORM_OF["ssd"], KX, lambda k: T["ysq"][:, k, :], T["ones_d"][:, :],
                            lambda k: pe.wait_ge(sem["ysq_ready"], k + 1))

            def rotate(j):
                n = (j + 1) % (PAIRS + 1)
                if n == 0:
                    pe.wait_ge(sem["seg_ready"], SSD_HEADS)
                else:
                    pe.wait_ge(sem["rope_read"], n)
                evacuated(pe, g_free, gn(("kr", 0) if j == PAIRS else ("q_rope", j)))
                pe.matmul(PT[:, 0:S], rot, T["rope_in"][:, j, :], start=True, stop=True
                          ).then_inc(sem["rot_full"], 1)

            def unit(u):
                n = NORM_OF["unit"] + u
                pe.wait_ge(sem["std_ready"], n)
                evacuated(pe, g_free, gn(("nope", u)))
                h = u % MLA_HEADS
                rows = slice(MLA_ROPE * (h % 2), MLA_ROPE * (h % 2 + 1))
                src = T["rope_sq"][:, h // 2 if u < MLA_HEADS else PAIRS, :]
                pe.matmul(NORM[:, 0:S], T["ones_h"][:, :], T["nope_sq"][:, u % 2, :], start=True, stop=False)
                pe.matmul(NORM[:, 0:S], T["ones_h"][rows, :], src[rows, :], start=False, stop=True
                          ).then_inc(sem["norm_full"], 1)

            def softmax(h):
                pe.wait_ge(sem["qk_ready"], MLA_HEADS + h + 1)
                if h == 0:
                    pe.wait_ge(sem["seg_ready"], SSD_HEADS)
                else:
                    pe.wait_ge(sem["exp_done"], TT * h)
                rows = slice(MLA_ROPE * (h % 2), MLA_ROPE * (h % 2 + 1))
                for t in range(TT):
                    q, n = slice(t * P, (t + 1) * P), (t + 1) * P
                    out = SC[:, t * S:t * S + n]
                    pe.matmul(out, T["nope"][:, h, q], T["nope"][:, MLA_HEADS + h, 0:n], start=True, stop=False)
                    pe.matmul(out, T["rope"][rows, h // 2, q], T["rope"][rows, PAIRS + h // 2, 0:n],
                              start=False, stop=False)
                    mm = pe.matmul(SC[:, t * S + t * P:t * S + n], ident, mask, start=False, stop=True)
                mm.then_inc(sem["s_full"], 1)

            def turn_probs(h):
                pe.wait_ge(sem["p_ready"], h + 1)
                if h == 0:
                    pe.wait_ge(sem["rope_read"], PAIRS + 1)
                else:
                    pe.wait_ge(sem["pt_ready"], h)
                for kt in range(TT):
                    for t in range(kt, TT):
                        mm = pe.transpose(PT[:, kt * S + t * P:kt * S + (t + 1) * P],
                                          T["probs"][:, h % 2, t, kt * P:(kt + 1) * P], ident)
                mm.then_inc(sem["pt_full"], 1)

            def values(h):
                pe.wait_ge(sem["pt_ready"], h + 1)
                evacuated(pe, g_free, gn(("v", h)))
                if h == 0:
                    pe.wait_ge(sem["y_read"], KX)
                else:
                    pe.wait_ge(sem["o_ready"], h)
                pe.matmul(OB[:, 0:S], T["v_tok"][:, 0, h, :], T["probsT"][:, h % 2, 0, :], start=True, stop=False)
                pe.matmul(OB[:, P:S], T["v_tok"][:, 1, h, :], T["probsT"][:, h % 2, 1, P:S], start=False,
                          stop=True).then_inc(sem["o_full"], 1)

            side = {"acum": acum, "cb": cb, "turn_x": turn_x, "decay": decay, "scan": scan,
                    "norm_cq": norm_cq, "norm_ckv": norm_ckv, "norm_ssd": norm_ssd, "rotate": rotate,
                    "unit": unit, "softmax": softmax, "turn_probs": turn_probs, "values": values}

            norm_x("ffn1", 0)
            ffn(H_FFN1, H_FFN1_OUT, 0)
            norm_x("mix", 1)
            for i, (kind, j) in enumerate(MIX_STEPS):
                g = gn((kind, j))
                if kind == "dt":
                    pe.wait_ge(sem["x_low_ready"], 2 * KD)
                    project_tok(g, lambda k, t: xm[:, k, t * P:(t + 1) * P], KD, SSD_HEADS)
                elif kind == "v":
                    project_tok(g, lambda k, t: T["lora"][:, KQ + k, t * P:(t + 1) * P], KC, P)
                elif kind in ("q_rope", "nope"):
                    query = kind == "q_rope" or j < MLA_HEADS
                    pe.wait_ge(sem["lora_ready"], KQ if query else KQ + KC)
                    project(g, (lambda k: T["lora"][:, k, :]) if query else
                            (lambda k: T["lora"][:, KQ + k, :]), KQ if query else KC)
                elif kind == "ssd_out":
                    pe.wait_ge(sem["ysq_ready"], KX)
                    project(g, lambda k: T["xs"][:, k, :], KX)
                elif kind == "mla_out":
                    pe.wait_ge(sem["o_ready"], MLA_HEADS)
                    project(g, lambda k: T["attn"][:, k, :], KD)
                elif kind == "out":
                    pe.wait_ge(sem["merged"], KD)
                    project(g, lambda k: T["merged"][:, k, :], KD)
                else:
                    project_halved(g, T["x_high"], T["x_low"], KD)
                for what, n in SIDE.get(i, []):
                    if what in side:
                        side[what](n)
            norm_x("ffn2", 2)
            ffn(H_FFN2, H_FFN2_OUT, 2)

        @block.scalar
        def _(act):
            chain = [0]

            def link(ins):
                chain[0] += 1
                ins.then_inc(sem["act_chain"], 1)
                act.wait_ge(sem["act_chain"], chain[0])

            def copy_out(g, out, func=ACT.Copy, **kw):
                act.wait_ge(g_full, g + 1)
                act.activation(out, G[:, g % GB, 0:S], func, **kw).then_inc(g_free[g % GB], 1)

            def cut(n, chunk):
                act.wait_ge(w_loaded[chunk % RING_2], 16 * (chunk // RING_2 + 1))
                if n >= PARTS:
                    act.wait_ge(sem["w_used"], HALVED_CHUNKS[n - PARTS] + 1)
                act.activation(T["w_high"][:, n % PARTS, :], ring[:, chunk % RING_2, :], ACT.Copy
                               ).then_inc(sem["high_ready"], 1)

            halves_of = Halves(act, cut)

            def squares(ready=None):
                for k in range(KD):
                    if ready:
                        ready(k)
                    act.activation(xm[:, k, :], x[:, k, :], ACT.Square).then_inc(sem["sq_ready"], 1)

            def x_high(i):
                for k in range(KD):
                    act.wait_ge(sem["xm_ready"], i * KD + k + 1)
                    act.activation(T["x_high"][:, k, :], xm[:, k, :], ACT.Copy
                                   ).then_inc(sem["x_high_ready"], 1)

            def root(n, scale=1.0):
                act.wait_ge(sem["norm_full"], n + 1)
                if n >= 1:
                    act.wait_ge(sem["rstd_ready"], n)
                act.activation(std[:, :], NORM[:, 0:S], ACT.Sqrt, bias=T["eps"][:, :], scale=scale
                               ).then_inc(sem["std_ready"], 1)

            def ffn(g0, g_out, i):
                def high(j):
                    evacuated(act, g_free, g0 + 2 * j + 1)
                    act.activation(ff_high[:, j, :], ff[:, j % 2, :], ACT.Copy).then_inc(sem["ff_high_ready"], 1)

                for j in range(KF):
                    halves_of.ahead(g0 + 2 * j)
                    if j >= 2:
                        evacuated(act, g_free, g0 + 2 * j - 3)
                    copy_out(g0 + 2 * j, silu[:, j % 2, :], ACT.Silu)
                    halves_of.ahead(g0 + 2 * j + 1)
                    if j >= 1:
                        high(j - 1)
                high(KF - 1)
                for j in range(KD):
                    halves_of.ahead(g_out + j)

            def conv_act(j):
                act.wait_ge(sem["conv_sum"], j + 1)
                out = T["bc"][:, j, :] if j < 2 * SSD_GROUPS else T["xs"][:, j - 2 * SSD_GROUPS, :]
                act.activation(out, T["conv"][:, j % 2, :], ACT.Silu).then_inc(sem["conv_done"], 1)

            def softplus(_):
                evacuated(act, g_free, gn(("dt", 0)))
                link(act.activation(T["soft"][:, :, :], T["dt"][:, :, :], ACT.Abs))
                link(act.activation(T["soft"][:, :, :], T["soft"][:, :, :], ACT.Exp, scale=-1.0))
                link(act.activation(T["soft"][:, :, :], T["soft"][:, :, :], ACT.Ln, bias=T["one"][:, :]))
                act.activation(T["a_exp"][:, :], p2("a_log"), ACT.Exp).then_inc(sem["soft_ready"], 1)

            def decay(h):
                act.wait_ge(sem["seg_ready"], h + 1)
                if h >= 2:
                    act.wait_ge(sem["m_ready"], h - 1)
                act.activation(T["decay"][:, h % 2, :], T["seg"][:, h % 2, :], ACT.Exp
                               ).then_inc(sem["decay_ready"], 1)

            def scan(j):
                act.wait_ge(sem["gated"], j + 1)
                act.activation(T["ysq"][:, j, :], T["z"][:, j, :], ACT.Square)
                act.activation(T["xs"][:, j, :], T["z"][:, j, :], ACT.Copy, scale=p2("ssd_norm")[:, j:j + 1]
                               ).then_inc(sem["ysq_ready"], 1)

            def softmax(h):
                act.wait_ge(sem["bias_ready"], h + 1)
                if h >= 2:
                    act.wait_ge(sem["pt_full"], h - 1)
                for t in range(TT):
                    n = (t + 1) * P
                    act.activation(T["probs"][:, h % 2, t, 0:n], SC[:, t * S:t * S + n], ACT.Exp,
                                   bias=T["nbias"][:, h, t:t + 1], scale=qk_scale,
                                   accum_out=T["rsum"][:, h, t:t + 1]).then_inc(sem["exp_done"], 1)

            def turn_probs(h):
                act.wait_ge(sem["pt_full"], h + 1)
                if h >= 2:
                    act.wait_ge(sem["o_full"], h - 1)
                act.activation(T["probsT"][:, h % 2, 0, :], PT[:, 0:S], ACT.Copy)
                act.activation(T["probsT"][:, h % 2, 1, P:S], PT[:, S + P:2 * S], ACT.Copy
                               ).then_inc(sem["pt_ready"], 1)

            def values(h):
                act.wait_ge(sem["o_full"], h + 1)
                act.activation(T["attn"][:, h, :], OB[:, 0:S], ACT.Copy).then_inc(sem["o_ready"], 1)

            side = {"acum": lambda _: None, "conv_act": conv_act, "decay": decay, "scan": scan,
                    "norm_cq": lambda _: root(NORM_OF["cq"], P / Q_LORA),
                    "norm_ckv": lambda _: root(NORM_OF["ckv"], P / KV_LORA),
                    "norm_ssd": lambda _: root(NORM_OF["ssd"], D / SSD_INNER),
                    "unit": lambda u: root(NORM_OF["unit"] + u, P / MLA_QK),
                    "softmax": softmax, "turn_probs": turn_probs, "values": values}

            squares()
            root(NORM_OF["ffn1"])
            x_high(0)
            ffn(H_FFN1, H_FFN1_OUT, 0)
            squares(lambda k: evacuated(act, g_free, H_FFN1_OUT + k))
            root(NORM_OF["mix"])
            x_high(1)
            act.wait_ge(sem["par_loaded"], 16)
            for i, (kind, j) in enumerate(MIX_STEPS):
                g = gn((kind, j))
                halves_of.ahead(g)
                if kind in ("bc", "xs"):
                    n = j + (2 * SSD_GROUPS if kind == "xs" else 0)
                    if n >= 2:
                        act.wait_ge(sem["conv_sum"], n - 1)
                    if n == 0:
                        act.wait_ge(sem["pads_ready"], 1)
                    copy_out(g, T["cpad"][:, n % 2, CONV - 1:])
                elif kind == "z":
                    copy_out(g, T["z"][:, j, :], ACT.Silu)
                elif kind in ("cq", "ckv"):
                    n = j + (KQ if kind == "ckv" else 0)
                    act.wait_ge(g_full, g + 1)
                    act.activation(T["lora_sq"][:, n, :], G[:, g % GB, 0:S], ACT.Square)
                    copy_out(g, T["lora_raw"][:, n, :])
                elif kind in ("kr", "q_rope"):
                    n = PAIRS if kind == "kr" else j
                    act.wait_ge(g_full, g + 1)
                    act.activation(T["rope_sq"][:, n, :], G[:, g % GB, 0:S], ACT.Square)
                    copy_out(g, T["rope_in"][:, n, :], scale=p2("k_rope" if kind == "kr" else "q_rope"))
                elif kind == "gate":
                    copy_out(g, T["gates"][:, j, :], ACT.Sigmoid)
                elif kind == "nope":
                    if j >= 2:
                        act.wait_ge(sem["norm_full"], NORM_OF["unit"] + j - 1)
                    act.wait_ge(g_full, g + 1)
                    act.activation(T["nope_sq"][:, j % 2, :], G[:, g % GB, 0:S], ACT.Square)
                    copy_out(g, T["nope"][:, j, :], scale=p2("q_nope" if j < MLA_HEADS else "k_nope"))
                elif kind == "v":
                    copy_out(g, T["v_tok"][:, :, j, :])
                if kind == "dt":
                    softplus(0)
                for what, n in SIDE.get(i, []):
                    if what in side:
                        side[what](n)
            squares(lambda k: evacuated(act, g_free, gn(("out", k))))
            root(NORM_OF["ffn2"])
            x_high(2)
            ffn(H_FFN2, H_FFN2_OUT, 1)

        @block.vector
        def _(dve):
            chain = [0]

            def link(ins):
                chain[0] += 1
                ins.then_inc(sem["dve_chain"], 1)
                dve.wait_ge(sem["dve_chain"], chain[0])

            def inverse_std(n, out=rstd):
                dve.wait_ge(sem["std_ready"], n + 1)
                dve.reciprocal(out[:, :], std[:, :]).then_inc(sem["rstd_ready"], 1)
                dve.wait_ge(sem["rstd_ready"], n + 1)

            def norm_x(n, weight, i):
                inverse_std(n)
                for k in range(KD):
                    dve.scalar_tensor_tensor(out=xm[:, k, :], in0=x[:, k, :], scalar=p2(weight)[:, k:k + 1],
                                             in1=rstd[:, :], op0=ALU.mult, op1=ALU.mult
                                             ).then_inc(sem["xm_ready"], 1)
                for k in range(KD):
                    dve.wait_ge(sem["xm_ready"], i * KD + k + 1)
                    dve.wait_ge(sem["x_high_ready"], i * KD + k + 1)
                    dve.tensor_tensor(T["x_low"][:, k, :], xm[:, k, :], T["x_high"][:, k, :].bitcast(F32),
                                      ALU.subtract).then_inc(sem["x_low_ready"], 1)

            def cut(n, chunk):
                dve.wait_ge(sem["high_ready"], n + 1)
                dve.tensor_tensor(T["w_low"][:, n % PARTS, :], ring[:, chunk % RING_2, :],
                                  T["w_high"][:, n % PARTS, :].bitcast(F32), ALU.subtract
                                  ).then_inc(sem["low_ready"], 1)

            halves_of = Halves(dve, cut)

            def ffn(g0, g_out, i):
                def low(j):
                    dve.wait_ge(sem["ff_high_ready"], i * KF + j + 1)
                    dve.tensor_tensor(ff_low[:, j, :], ff[:, j % 2, :], ff_high[:, j, :].bitcast(F32),
                                      ALU.subtract).then_inc(sem["ff_low_ready"], 1)

                for j in range(KF):
                    g = g0 + 2 * j
                    halves_of.ahead(g)
                    halves_of.ahead(g + 1)
                    if j >= 1:
                        low(j - 1)
                    if j >= 2:
                        dve.wait_ge(sem["ff_low_ready"], i * KF + j - 1)
                    evacuated(dve, g_free, g)
                    dve.wait_ge(g_full, g + 2)
                    dve.tensor_tensor(ff[:, j % 2, :], G[:, (g + 1) % GB, 0:S], silu[:, j % 2, :], ALU.mult
                                      ).then_inc(g_free[(g + 1) % GB], 1)
                    evacuated(dve, g_free, g + 1)
                low(KF - 1)
                for j in range(KD):
                    g = g_out + j
                    halves_of.ahead(g)
                    dve.wait_ge(g_full, g + 1)
                    dve.scalar_tensor_tensor(out=x[:, j, :], in0=G[:, g % GB, 0:S], scalar=0.5,
                                             in1=x[:, j, :], op0=ALU.mult, op1=ALU.add
                                             ).then_inc(g_free[g % GB], 1)

            def dt_bias():
                g = gn(("dt", 0))
                dve.wait_ge(g_full, g + 1)
                dve.tensor_tensor(T["dt"][:, :, :], halves(G[:, g % GB, 0:S])[:, :, 0:SSD_HEADS],
                                  p2("dt_bias").unsqueeze(1).to_broadcast([P, TT, SSD_HEADS]), ALU.add
                                  ).then_inc(g_free[g % GB], 1)
                evacuated(dve, g_free, g)
                dve.wait_ge(sem["soft_ready"], 1)
                link(dve.scalar_tensor_tensor(out=T["dt"][:, :, :], in0=T["dt"][:, :, :], scalar=0.0,
                                              in1=T["soft"][:, :, :], op0=ALU.max, op1=ALU.add))
                dve.scalar_tensor_tensor(out=T["dta"][:, :, :], in0=T["dt"][:, :, :], scalar=-1.0,
                                         in1=T["a_exp"][:, :].unsqueeze(1).to_broadcast([P, TT, SSD_HEADS]),
                                         op0=ALU.mult, op1=ALU.mult).then_inc(sem["dta_ready"], 1)

            def acum(_):
                dve.wait_ge(sem["acum_full"], 1)
                dve.tensor_copy(T["acum_t"][:, :, :], NORM[:, 0:2 * SSD_HEADS].rearrange("p (a h) -> p a h", a=2))
                dve.tensor_copy(T["acum_h"][:, :], NORM[0:SSD_HEADS, S:2 * S]).then_inc(sem["acum_ready"], 1)

            def conv(j):
                kind = ("bc", j) if j < 2 * SSD_GROUPS else ("xs", j - 2 * SSD_GROUPS)
                evacuated(dve, g_free, gn(kind))
                if j >= 2:
                    dve.wait_ge(sem["conv_done"], j - 1)
                pad, out = T["cpad"][:, j % 2, :], T["conv"][:, j % 2, :]
                wj = p2("conv_w")[:, j * CONV:(j + 1) * CONV]
                link(dve.tensor_scalar(out, pad[:, 0:S], wj[:, 0:1], p2("conv_b")[:, j:j + 1], ALU.mult,
                                       ALU.add))
                for tap in range(1, CONV):
                    ins = dve.scalar_tensor_tensor(out=out, in0=pad[:, tap:tap + S], scalar=wj[:, tap:tap + 1],
                                                   in1=out, op0=ALU.mult, op1=ALU.add)
                    if tap < CONV - 1:
                        link(ins)
                ins.then_inc(sem["conv_sum"], 1)

            def cb(g):
                dve.wait_ge(sem["cb_full"], g + 1)
                dve.tensor_tensor(T["cb"][:, g, 0:S], PT[:, 0:S], tri, ALU.mult)
                dve.tensor_tensor(T["cb"][:, g, S:S + P], PT[:, S:S + P], tri[:, 0:P], ALU.mult
                                  ).then_inc(sem["cb_ready"], 1)

            def turn_x(j):
                g = TURN_X[j]
                dve.wait_ge(g_full, g + 1)
                dve.tensor_tensor(
                    T["xdt"][:, :, j * P:(j + 1) * P].rearrange("p a (h d) -> p a h d", h=2),
                    G[:, g % GB, 0:S].rearrange("p (a h d) -> p a h d", a=TT, h=2),
                    T["dt"][:, :, 2 * j:2 * j + 2].unsqueeze(3).to_broadcast([P, TT, 2, SSD_HEAD_DIM]), ALU.mult
                ).then_inc(g_free[g % GB], 1)

            def decay(h):
                dve.wait_ge(sem["row_full"], h + 1)
                if h == 0:
                    dve.wait_ge(sem["acum_ready"], 1)
                    dve.wait_ge(sem["cb_ready"], SSD_GROUPS)
                if h >= 2:
                    dve.wait_ge(sem["decay_ready"], h - 1)
                row = (SC, PT)[h % 2]
                dve.tensor_scalar(T["seg"][:, h % 2, 0:S], row[:, 0:S], T["acum_t"][:, 0, h:h + 1], 0.0,
                                  ALU.subtract, ALU.min)
                dve.tensor_scalar(T["seg"][:, h % 2, S:S + P], row[:, P:S],
                                  T["acum_t"][:, 1, h:h + 1], 0.0, ALU.subtract, ALU.min
                                  ).then_inc(sem["seg_ready"], 1)
                dve.wait_ge(sem["decay_ready"], h + 1)
                if h >= 4:
                    dve.wait_ge(sem["y_full"], h // 2 - 1)
                dve.tensor_tensor(T["m"][:, h % 4, :], T["decay"][:, h % 2, :], T["cb"][:, h // HPG, :], ALU.mult
                                  ).then_inc(sem["m_ready"], 1)

            def scan(j):
                dve.wait_ge(sem["y_full"], j + 1)
                if j >= 2:
                    dve.wait_ge(sem["gated"], j - 1)
                dve.scalar_tensor_tensor(out=T["y"][:, j % 2, :], in0=T["xs"][:, j, :],
                                         scalar=p2("d_skip")[:, j:j + 1], in1=OB[:, 0:S], op0=ALU.mult,
                                         op1=ALU.add).then_inc(sem["y_read"], 1)
                dve.wait_ge(sem["y_read"], j + 1)
                evacuated(dve, g_free, gn(("z", j)))
                dve.tensor_tensor(T["z"][:, j, :], T["y"][:, j % 2, :], T["z"][:, j, :], ALU.mult
                                  ).then_inc(sem["gated"], 1)

            def norm_lora(n, at, count, weight):
                inverse_std(n)
                for k in range(count):
                    dve.scalar_tensor_tensor(out=T["lora"][:, at + k, :], in0=T["lora_raw"][:, at + k, :],
                                             scalar=p2(weight)[:, k:k + 1], in1=rstd[:, :], op0=ALU.mult,
                                             op1=ALU.mult).then_inc(sem["lora_ready"], 1)
                dve.wait_ge(sem["lora_ready"], at + count)

            def rotate(j):
                n = (j + 1) % (PAIRS + 1)
                dve.wait_ge(sem["rot_full"], n + 1)
                dve.tensor_tensor(T["rope2"][:, :], PT[:, 0:S], T["sin2"][:, :], ALU.mult
                                  ).then_inc(sem["rope_read"], 1)
                dve.wait_ge(sem["rope_read"], n + 1)
                link(dve.tensor_tensor(T["rope_out"][:, j, :], T["rope_in"][:, j, :], T["cos2"][:, :], ALU.mult))
                link(dve.tensor_tensor(T["rope_out"][:, j, :], T["rope_out"][:, j, :], T["rope2"][:, :],
                                       ALU.add))

            def unit(u):
                inverse_std(NORM_OF["unit"] + u)
                h = u % MLA_HEADS
                rows = slice(MLA_ROPE * (h % 2), MLA_ROPE * (h % 2 + 1))
                src, dst = (h // 2, h // 2) if u < MLA_HEADS else (PAIRS, PAIRS + h // 2)
                link(dve.tensor_tensor(T["rope"][rows, dst, :], T["rope_out"][rows, src, :], rstd[rows, :],
                                       ALU.mult))
                dve.tensor_tensor(T["nope"][:, u, :], T["nope"][:, u, :], rstd[:, :], ALU.mult
                                  ).then_inc(sem["qk_ready"], 1)
                dve.wait_ge(sem["qk_ready"], u + 1)

            def softmax(h):
                dve.wait_ge(sem["s_full"], h + 1)
                for t in range(TT):
                    ins = dve.tensor_reduce(T["smax"][:, h, t:t + 1], SC[:, t * S:t * S + (t + 1) * P], AX_X,
                                            ALU.max)
                link(ins)
                dve.tensor_scalar(T["nbias"][:, h, :], T["smax"][:, h, :], -qk_scale, None, ALU.mult
                                  ).then_inc(sem["bias_ready"], 1)
                dve.wait_ge(sem["exp_done"], TT * (h + 1))
                link(dve.reciprocal(T["rinv"][:, h, :], T["rsum"][:, h, :]))
                for t in range(TT):
                    n = (t + 1) * P
                    ins = dve.tensor_scalar(T["probs"][:, h % 2, t, 0:n], T["probs"][:, h % 2, t, 0:n],
                                            T["rinv"][:, h, t:t + 1], None, ALU.mult)
                ins.then_inc(sem["p_ready"], 1)

            side = {"acum": acum, "conv": conv, "cb": cb, "turn_x": turn_x, "decay": decay, "scan": scan,
                    "norm_cq": lambda _: norm_lora(NORM_OF["cq"], 0, KQ, "q_lora"),
                    "norm_ckv": lambda _: norm_lora(NORM_OF["ckv"], KQ, KC, "kv_lora"),
                    "norm_ssd": lambda _: inverse_std(NORM_OF["ssd"], T["rstd_ssd"]),
                    "rotate": rotate, "unit": unit, "softmax": softmax}

            dve.memset(T["cpad"][:, :, 0:CONV - 1], 0.0).then_inc(sem["pads_ready"], 1)
            dve.wait_ge(sem["par_loaded"], 16)
            norm_x(NORM_OF["ffn1"], "ln_ffn1", 0)
            ffn(H_FFN1, H_FFN1_OUT, 0)
            norm_x(NORM_OF["mix"], "ln_mix", 1)
            for i, (kind, j) in enumerate(MIX_STEPS):
                g = gn((kind, j))
                halves_of.ahead(g)
                if kind == "dt":
                    dt_bias()
                elif kind == "ssd_out":
                    dve.wait_ge(g_full, g + 1)
                    evacuated(dve, g_free, gn(("gate", j)))
                    dve.tensor_tensor(T["merged"][:, j, :], G[:, g % GB, 0:S], T["rstd_ssd"][:, :], ALU.mult
                                      ).then_inc(g_free[g % GB], 1)
                    evacuated(dve, g_free, g)
                    link(dve.tensor_tensor(T["merged"][:, j, :], T["merged"][:, j, :], T["gates"][:, j, :],
                                           ALU.mult))
                elif kind == "mla_out":
                    dve.wait_ge(g_full, g + 1)
                    evacuated(dve, g_free, gn(("gate", KD + j)))
                    dve.tensor_tensor(T["y"][:, j % 2, :], G[:, g % GB, 0:S], T["gates"][:, KD + j, :], ALU.mult
                                      ).then_inc(g_free[g % GB], 1)
                    evacuated(dve, g_free, g)
                    dve.tensor_tensor(T["merged"][:, j, :], T["merged"][:, j, :], T["y"][:, j % 2, :], ALU.add
                                      ).then_inc(sem["merged"], 1)
                    dve.wait_ge(sem["merged"], j + 1)
                elif kind == "out":
                    dve.wait_ge(g_full, g + 1)
                    dve.tensor_tensor(x[:, j, :], G[:, g % GB, 0:S], x[:, j, :], ALU.add
                                      ).then_inc(g_free[g % GB], 1)
                for what, n in SIDE.get(i, []):
                    if what in side:
                        side[what](n)
            norm_x(NORM_OF["ffn2"], "ln_ffn2", 2)
            ffn(H_FFN2, H_FFN2_OUT, 1)


NSEM_1 = ("par_loaded", "w_used", "g_full", "ada_full", "sq_ready", "norm_full", "std_ready", "rstd_ready",
          "xn_ready", "xm_ready", "rope_read", "qk_ready", "s_full", "bias_ready", "exp_done", "p_ready",
          "pt_full", "pt_ready", "o_full", "o_ready", "pads_ready", "pooled", "merged", "top_ready",
          "gate_exp", "routed", "u_used", "v_used", "gelu_done", "weight_ready", "diag_ready", "y_copied",
          "dve_chain", "act_chain")
NSEM_2 = ("dta_ready", "acum_full", "acum_ready", "conv_sum", "conv_done", "cb_full", "cb_ready",
          "row_full", "seg_ready", "decay_ready", "m_ready", "y_full", "y_read", "gated", "ysq_ready",
          "lora_ready", "rot_full", "soft_ready", "high_ready", "low_ready", "x_high_ready",
          "x_low_ready", "ff_high_ready", "ff_low_ready")


def program(nc, io, models=(1, 2), depth=DEPTH):
    with ExitStack() as ctx:
        def sb(name, shape, dt=F32, scope=ctx):
            return scope.enter_context(nc.sbuf_tensor(name, shape, dt))

        def part(tile, at, *shape):
            n = int(np.prod(shape))
            flat = tile[:, at:at + n]
            if len(shape) == 1:
                return flat
            names = "abc"[:len(shape)]
            return flat.rearrange(f"p ({' '.join(names)}) -> p {' '.join(names)}",
                                  **dict(zip(names, shape)))

        T = {k: io[k] for k in ("stream1", "stream2", "par1", "par2", "expert_u", "expert_v")}
        T["x"] = sb("x", [P, KD, S])
        T["const"] = sb("const", [P, NCONST])
        T["par"] = sb("par", [P, max(NPAR_1, NPAR_2)])
        T["std"], T["rstd"] = sb("std", [P, S]), sb("rstd", [P, S])
        T["ones_d"], T["ones_h"] = sb("ones_d", [P, P]), sb("ones_h", [P, P])
        T["eps"], T["one"] = sb("eps", [P, 1]), sb("one", [P, 1])
        T["cos2"], T["sin2"] = sb("cos2", [P, S]), sb("sin2", [P, S])
        T["c_act"] = sb("c_act", [P, KD])
        T["final_w"] = sb("final_w", [P, KD])
        T["first_expert"] = sb("first_expert", [P, 1])
        T["G"] = ctx.enter_context(nc.psum_tensor("G", [P, GB, 512], F32))
        T["M"] = ctx.enter_context(nc.psum_tensor("M", [P, 4, 512], F32))
        sem = {n: ctx.enter_context(nc.semaphore(n)) for n in NSEM_1 + NSEM_2 + ("io_loaded", "setup", "stored")}
        for name, n in (("w_loaded", RING), ("g_free", GB), ("u_landed", SLOTS), ("v_landed", SLOTS)):
            sem[name] = [ctx.enter_context(nc.semaphore(f"{name}{i}")) for i in range(n)]

        def clear():
            nc.all_engine_barrier()
            nc.gpsimd.dma_reset()
            nums = sorted(one.num for s in sem.values() for one in (s if isinstance(s, list) else [s]))
            assert nums == list(range(nums[0], nums[-1] + 1))
            nc.gpsimd.sem_clear(range(nums[0], nums[-1] + 1))
            nc.all_engine_barrier()

        x = T["x"]
        with ExitStack() as first:
            c_in = sb("c_in", [P, KD], scope=first)
            with nc.Block() as block:
                @block.sync
                def _(sp):
                    sp.dma_start(c_in[:, :], io["c"]).then_inc(sem["io_loaded"], 16)
                    sp.dma_start(x[:, :, :], io["x"]).then_inc(sem["stored"], 16)
                    sp.dma_start(T["const"][:, :], io["const"]).then_inc(sem["stored"], 16)
                    sp.dma_start(T["final_w"][:, :], io["final_w"]).then_inc(sem["stored"], 16)
                    sp.wait_ge(sem["stored"], 48)

                @block.vector
                def _(dve):
                    dve.memset(T["ones_d"][:, :], 1.0 / D)
                    dve.memset(T["ones_h"][:, :], 1.0 / P)
                    dve.memset(T["eps"][:, :], EPS)
                    dve.memset(T["one"][:, :], 1.0)
                    dve.memset(T["first_expert"][:, :], 0.0)

                @block.scalar
                def _(act):
                    act.wait_ge(sem["io_loaded"], 16)
                    act.activation(T["c_act"][:, :], c_in[:, :], ACT.Silu)

        if 1 in models:
            with ExitStack() as first:
                def sb1(name, *shape, dt=F32):
                    return sb(name, [P, *shape], dt, first)

                ua, va = sb1("u_rows", SLOTS * D), sb1("v_rows", SLOTS * D)
                T["u_rows"], T["v_rows"] = part(ua, 0, SLOTS, D), part(va, 0, SLOTS, D)
                T["qk"] = part(ua, 0, UNITS, S)
                T["probs"] = part(ua, 2560, 2, TT, S)
                T["probsT"] = part(ua, 3584, 2, TT, S)
                T["merged"] = part(ua, 4608, KD, S)
                T["v_tok"] = part(ua, 6656, TT, KV_HEADS, P)
                T["qsq"], T["qw"] = part(ua, 7168, 2, S), part(ua, 7680, 2, S)
                T["xn"] = part(va, 0, KD, S)
                T["pooled"], T["mixed"] = part(va, 2048, 4, S), part(va, 3072, 4, S)
                T["upad"] = part(va, 4096, 4, S + 2 * PADW)
                T["win"] = part(va, 5184, 2, S + 2 * PADW)
                T["sq"], T["xm"] = sb1("sq", KD, S), sb1("xm", KD, S)
                T["ring"] = sb1("ring", RING, TILES * P)
                T["rope1"], T["rope2"] = sb1("rope1", S), sb1("rope2", S)
                att = sb1("attn", KD * S)
                T["attn"], T["x_tok"] = part(att, 0, KD, S), part(att, 0, TT, D)
                gates = sb1("gates", 2 * KD * S)
                T["gates"], T["key_score"] = part(gates, 0, 2 * KD, S), part(gates, 0, PEER_HEADS, 4 * P)
                query = sb1("query", 2 * 4 * S)
                T["query"], T["y_tok"] = part(query, 0, 2, 4, S), part(query, 0, TT, D)
                T["diag"] = sb1("diag", 4, P)
                T["mod"], T["scale1"] = sb1("mod", N_ADA * KD), sb1("scale1", 2, KD)
                for name in ("smax", "nbias", "rsum", "rinv"):
                    T[name] = sb1(name, HEADS, TT)
                T["val"], T["idx"] = sb1("val", 2, TOPK), sb1("idx", 2, TOPK, dt=U32)
                T["idxf"], T["rest"] = sb1("idxf", 2, TOPK), sb1("rest", TOPK * TOPK)
                T["cand"], T["pos"] = sb1("cand", TOPK * TOPK), sb1("pos", TOPK, dt=U32)
                T["pos_ij"], T["pos_f"] = sb1("pos_ij", 2, TOPK, dt=U32), sb1("pos_f", 2, TOPK)
                T["pick"], T["key"] = sb1("pick", TOPK, TOPK), sb1("key", 2, TOPK)
                for name in ("top", "gate", "hid", "gelu", "weight"):
                    T[name] = sb1(name, ROUNDS, TOPK)
                T["expert"] = sb1("expert", ROUNDS, TOPK, dt=U32)
                for name in ("neg_top", "gate_sum", "gate_inv"):
                    T[name] = sb1(name, ROUNDS)
                with nc.Fori(0, depth) as layer:
                    clear()
                    first_layer(nc, layer, T, sem)

                clear()
                final_norm(nc, T, sem)

        if 2 in models:
            with ExitStack() as tables:
                clear()
                rope_tables(nc, T, sem, io, sb("positions", [P, S], I32, tables))
            with ExitStack() as second:
                second_scope = second

                def sb2(name, *shape, dt=F32):
                    return sb(name, [P, *shape], dt, second_scope)

                T["ring"] = sb2("ring_2", RING_2, TILES * P)
                T["w_high"] = sb2("w_high", PARTS, TILES * P, dt=F32R)
                T["w_low"] = sb2("w_low", PARTS, TILES * P, dt=F32R)
                T["x_high"], T["x_low"] = sb2("x_high", KD, S, dt=F32R), sb2("x_low", KD, S, dt=F32R)

                with ExitStack() as scope_ffn:
                    second_scope = scope_ffn
                    T["ff_high"], T["ff_low"] = sb2("ff_high", KF, S, dt=F32R), sb2("ff_low", KF, S, dt=F32R)
                    T["silu"], T["ff"] = sb2("silu", 2, S), sb2("ff", 2, S)
                    T["xm"] = sb2("squares_2", KD, S)
                with ExitStack() as scope_mix:
                    second_scope = scope_mix
                    att = sb2("attn2", KD * S)
                    T["attn"] = part(att, 0, KD, S)
                    xc = sb2("xdt_cb", TT * SSD_INNER + SSD_GROUPS * 3 * P)
                    T["xdt"], T["cb"] = part(xc, 0, TT, SSD_INNER), part(xc, TT * SSD_INNER, SSD_GROUPS, 3 * P)
                    T["v_tok"], T["merged"] = part(xc, 0, TT, MLA_HEADS, P), part(xc, 2048, KD, S)
                    T["lora"] = part(xc, TT * SSD_INNER, KQ + KC, S)
                    gates = sb2("gates2", 2 * KD * S)
                    T["gates"] = T["ysq"] = part(gates, 0, 2 * KD, S)
                    z = sb2("z", 2 * KD * S)
                    T["z"] = T["nope"] = part(z, 0, 2 * KD, S)
                    bc = sb2("bc", 2 * SSD_GROUPS * S)
                    T["bc"], T["lora_raw"] = part(bc, 0, 2 * SSD_GROUPS, S), part(bc, 0, KQ + KC, S)
                    T["xs"] = sb2("xs", KX, S)
                    work = sb2("work", 4220)
                    T["seg"], T["decay"], T["m"] = (part(work, 0, 2, 3 * P), part(work, 6 * P, 2, 3 * P),
                                                    part(work, 12 * P, 4, 3 * P))
                    T["conv"], T["cpad"] = part(work, 24 * P, 2, S), part(work, 24 * P + 2 * S, 2, CONV - 1 + S)
                    for n, name in enumerate(("rope_in", "rope_sq", "rope_out")):
                        T[name] = part(work, n * (PAIRS + 1) * S, PAIRS + 1, S)
                    T["probs"], T["probsT"] = part(work, 0, 2, TT, S), part(work, 4 * S, 2, TT, S)
                    rope = sb2("rope", 2 * PAIRS * S)
                    T["rope"], T["lora_sq"] = part(rope, 0, 2 * PAIRS, S), part(rope, 0, KQ + KC, S)
                    y = sb2("y2", 2 * S)
                    T["y"] = T["nope_sq"] = part(y, 0, 2, S)
                    T["rope2"] = sb2("rope2b", S)
                    T["rstd_ssd"] = sb2("rstd_ssd", S)
                    for name in ("dt", "dta", "soft", "acum_t"):
                        T[name] = sb2(name, TT, SSD_HEADS)
                    T["a_exp"] = sb2("a_exp", SSD_HEADS)
                    T["acum_h"] = T["rope2"][0:SSD_HEADS, :]
                    for name in ("smax", "nbias", "rsum", "rinv"):
                        T[name] = sb2(name + "2", MLA_HEADS, TT)
                with nc.Fori(0, depth) as layer:
                    clear()
                    second_layer(nc, layer, T, sem)

        clear()
        with nc.Block() as block:
            @block.sync
            def _(sp):
                sp.dma_start(io["out"], x[:, :, :]).then_inc(sem["stored"], 16)
                sp.wait_ge(sem["stored"], 16)


def final_norm(nc, T, sem):
    x, xm, M = T["x"], T["sq"], T["M"]
    with nc.Block() as block:
        @block.scalar
        def _(act):
            for k in range(KD):
                act.activation(xm[:, k, :], x[:, k, :], ACT.Square).then_inc(sem["sq_ready"], 1)
            act.wait_ge(sem["norm_full"], 1)
            act.activation(T["std"][:, :], M[:, 0, 0:S], ACT.Sqrt, bias=T["eps"][:, :]
                           ).then_inc(sem["std_ready"], 1)

        @block.tensor
        def _(pe):
            for k in range(KD):
                pe.wait_ge(sem["sq_ready"], k + 1)
                mm = pe.matmul(M[:, 0, 0:S], T["ones_d"][:, :], xm[:, k, :], start=(k == 0), stop=(k == KD - 1))
            mm.then_inc(sem["norm_full"], 1)

        @block.vector
        def _(dve):
            dve.wait_ge(sem["std_ready"], 1)
            dve.reciprocal(T["rstd"][:, :], T["std"][:, :]).then_inc(sem["rstd_ready"], 1)
            dve.wait_ge(sem["rstd_ready"], 1)
            for k in range(KD):
                dve.scalar_tensor_tensor(out=x[:, k, :], in0=x[:, k, :], scalar=T["final_w"][:, k:k + 1],
                                         in1=T["rstd"][:, :], op0=ALU.mult, op1=ALU.mult)


TWO_PI = 6.283185307179586
TWO_PI_PARTS = (6.28125, 0.0019350051879882812, 3.019917368e-07)
ROUND = 12582912.0
PI_BELOW = 3.1415925


def rope_tables(nc, T, sem, io, pos):
    cos2, sin2, ang, turns = T["cos2"], T["sin2"], T["std"], T["rstd"]
    inv = columns(T["const"], CONST, "inv_freq")
    with nc.Block() as block:
        @block.sync
        def _(sp):
            sp.dma_start(pos[:, :], io["positions"].to_broadcast([P, S])).then_inc(sem["io_loaded"], 16)
            sp.wait_ge(sem["io_loaded"], 16)

        @block.vector
        def _(dve):
            chain = [0]

            def link(ins):
                chain[0] += 1
                ins.then_inc(sem["dve_chain"], 1)
                dve.wait_ge(sem["dve_chain"], chain[0])

            dve.wait_ge(sem["io_loaded"], 16)
            link(dve.tensor_copy(ang[:, :], pos[:, :]))
            link(dve.tensor_scalar(ang[:, :], ang[:, :], inv, None, ALU.mult))
            for out, quarter in ((sin2, 0.0), (cos2, 0.25)):
                link(dve.tensor_scalar(turns[:, :], ang[:, :], 1.0 / TWO_PI, quarter, ALU.mult, ALU.add))
                link(dve.tensor_scalar(turns[:, :], turns[:, :], ROUND, None, ALU.add))
                link(dve.tensor_scalar(turns[:, :], turns[:, :], ROUND, None, ALU.subtract))
                link(dve.tensor_copy(out[:, :], ang[:, :]))
                for p in TWO_PI_PARTS:
                    link(dve.scalar_tensor_tensor(out=out[:, :], in0=turns[:, :], scalar=-p, in1=out[:, :],
                                                  op0=ALU.mult, op1=ALU.add))
                link(dve.tensor_scalar(out[:, :], out[:, :], quarter * TWO_PI, PI_BELOW, ALU.add, ALU.min))
                dve.tensor_scalar(out[:, :], out[:, :], -PI_BELOW, None, ALU.max).then_inc(sem["setup"], 1)
                dve.wait_ge(sem["setup"], 1 if out is sin2 else 2)

        @block.scalar
        def _(act):
            for n, out in enumerate((sin2, cos2)):
                act.wait_ge(sem["setup"], n + 1)
                act.activation(out[:, :], out[:, :], ACT.Sin)


def _tiles(w):
    d, k, n = w.shape
    return w.reshape(d, k // P, P, n // P, P).transpose(0, 3, 1, 2, 4)


def _flat(t):
    return t.reshape(t.shape[0], -1, P, P)


def _stream(parts, chunks):
    depth = parts[0].shape[0]
    n = sum(p.shape[1] for p in parts)
    out = np.zeros((depth, chunks * TILES, P, P), parts[0].dtype)
    at = 0
    for p in parts:
        out[:, at:at + p.shape[1]] = p
        at += p.shape[1]
    assert at == n and -(-n // TILES) == chunks
    return np.ascontiguousarray(out.reshape(depth * chunks, TILES, P, P).transpose(0, 2, 1, 3)
                                ).reshape(depth * chunks, P, TILES * P)


def _features(v):
    return v.reshape(v.shape[0], -1, P).transpose(0, 2, 1)


def _params(table, parts, dtype):
    n = sum(k for _, k in table.values())
    out = np.zeros((DEPTH, P, n), dtype)
    for name, value in parts.items():
        at, k = table[name]
        out[:, :, at:at + k] = value
    return out


def _constants():
    out = np.zeros((P, NCONST), np.float32)

    def put(name, value):
        at, n = CONST[name]
        out[:, at:at + n] = value

    p, t = np.arange(P), np.arange(S)
    put("ident", np.eye(P))
    rot = np.zeros((P, P))
    for m in range(P):
        if m % 64 < 32:
            rot[m + 32, m] = -1.0
        else:
            rot[m - 32, m] = 1.0
    put("rot", rot)
    inv = (1.0 / (np.float32(10000.0) ** (np.arange(0, 64, 2, dtype=np.float32) / np.float32(64)))
           ).astype(np.float32)
    where = np.where((p < 64)[:, None], (t // 64)[None, :], (t % 64)[None, :]).astype(np.float32)
    ang = where * inv[p % 32][:, None]
    put("cos", np.cos(ang))
    put("sin", np.sin(ang))
    cnt = [np.clip(t + w // 2, 0, S) - np.clip(t - w // 2, 0, S) for w in POOL_WINDOWS]
    put("inv_cnt", (1.0 / np.concatenate(cnt))[None, :])
    put("iota", np.arange(TOPK)[None, :])
    put("tri", p[:, None] <= t[None, :])
    put("mask", np.where(p[None, :] <= p[:, None], 0.0, -1.0e30))
    put("inv_freq", inv[p % 32][:, None])
    return out


def lay_out(i):
    a = {k: np.asarray(v) for k, v in i.items()}
    f = np.float32
    ada = _tiles(a["ada_w"])
    w_in = a["w_in"]
    q, kv, rest = w_in[:, :, :D], w_in[:, :, D:D + 4 * P], w_in[:, :, D + 4 * P:]
    tin = _tiles(np.concatenate([kv, q, rest], 2))
    parts = [_flat(ada[:, :2 * KD])]
    for n in range(T_IN):
        parts += [tin[:, n], ada[:, 2 * KD + n]]
    parts += [a["pool_mix_w"], _flat(_tiles(a["w_pool_o"])), _flat(_tiles(a["w_attn_o"])),
              _flat(_tiles(a["w_out"]))]
    wq = _tiles(a["w_query"])
    keys = a["sub_keys"].transpose(0, 1, 2, 4, 3).reshape(DEPTH, PEER_HEADS, 4, P, P)
    for h in range(PEER_HEADS):
        parts += [_flat(wq[:, 4 * h:4 * h + 4]), keys[:, h]]
    stream1 = _stream(parts, CHUNKS_1)
    par1 = _params(PAR_1, {
        "ada_b": _features(a["ada_b"]), "norm_mix": _features(a["norm_mix_w"]),
        "norm_ffn": _features(a["norm_ffn_w"]), "q_norm": _features(a["q_norm_w"]),
        "k_norm": _features(a["k_norm_w"]), "pool_scale": _features(a["pool_scale"])}, f)

    def ffn(w13, w2):
        t = _tiles(w13)
        return [np.stack([t[:, :KF], t[:, KF:]], 2).reshape(DEPTH, -1, P, P), _flat(_tiles(w2))]

    w = a["w_in_2"]
    cut = np.cumsum([0, SSD_INNER, SSD_INNER + 2 * SSD_GROUPS * P, SSD_HEADS, Q_LORA, KV_LORA, MLA_ROPE, 2 * D])
    wz, wxbc, wdt, wcq, wckv, wkr, wg = (w[:, :, lo:hi] for lo, hi in zip(cut[:-1], cut[1:]))
    wdt = np.concatenate([wdt] + [np.zeros_like(wdt)] * 3, 2)
    uq = a["w_uq_2"].reshape(DEPTH, Q_LORA, MLA_HEADS, MLA_QK)
    uq_nope = _tiles(uq[..., :P].reshape(DEPTH, Q_LORA, -1))
    uq_rope = _tiles(uq[..., P:].reshape(DEPTH, Q_LORA, -1))
    ukv = a["w_ukv_2"].reshape(DEPTH, KV_LORA, MLA_HEADS, 2, P)
    uk, uv = (_tiles(ukv[..., n, :].reshape(DEPTH, KV_LORA, -1)) for n in range(2))
    gate = _tiles(wg)
    parts = ffn(a["ffn1_w13_2"], a["ffn1_w2_2"])
    parts += [_flat(_tiles(m)) for m in (wdt, wxbc[:, :, SSD_INNER:], wxbc[:, :, :SSD_INNER], wz, wcq, wckv,
                                         np.concatenate([wkr, wkr], 2))]
    parts += [_flat(uq_rope)]
    for n in range(2 * KD):
        parts += [gate[:, n], uq_nope[:, n] if n < MLA_HEADS else uk[:, n - MLA_HEADS]]
    parts += [_flat(uv), _flat(_tiles(a["w_ssd_out_2"])), _flat(_tiles(a["w_mla_out_2"])),
              _flat(_tiles(a["w_o_2"]))]
    parts += ffn(a["ffn2_w13_2"], a["ffn2_w2_2"])
    stream2 = _stream(parts, CHUNKS_2)

    def bc_first(v):
        return np.concatenate([v[..., SSD_INNER:], v[..., :SSD_INNER]], -1)

    def twice(v):
        return np.concatenate([v, v], 1)[:, :, None]

    conv_w = bc_first(a["conv_w_2"]).reshape(DEPTH, CONV, 24, P).transpose(0, 3, 2, 1).reshape(DEPTH, P, -1)
    par2 = _params(PAR_2, {
        "ln_ffn1": _features(a["ln_ffn1_2"]), "ln_mix": _features(a["ln_mix_2"]),
        "ln_ffn2": _features(a["ln_ffn2_2"]), "conv_w": conv_w,
        "conv_b": _features(bc_first(a["conv_b_2"])),
        "d_skip": _features(np.repeat(a["d_skip_2"], SSD_HEAD_DIM, 1)),
        "ssd_norm": _features(a["ssd_norm_2"]), "q_lora": _features(a["q_lora_norm_2"]),
        "kv_lora": _features(a["kv_lora_norm_2"]),
        "q_nope": a["q_norm_2"][:, :P, None], "q_rope": twice(a["q_norm_2"][:, P:]),
        "k_nope": a["k_norm_2"][:, :P, None], "k_rope": twice(a["k_norm_2"][:, P:]),
        "a_log": a["a_log_2"][:, None, :], "dt_bias": a["dt_bias_2"][:, None, :]}, f)
    return {
        "x": np.ascontiguousarray(a["x"][0].reshape(S, KD, P).transpose(2, 1, 0)),
        "c": np.ascontiguousarray(a["c"][0].reshape(KD, P).T),
        "const": _constants(),
        "final_w": np.ascontiguousarray(a["final_norm_w"].reshape(KD, P).T),
        "stream1": stream1, "par1": par1, "stream2": stream2, "par2": par2,
        "expert_u": np.ascontiguousarray(a["expert_u"]).reshape(DEPTH * N_EXPERTS, D),
        "expert_v": np.ascontiguousarray(a["expert_v"]).reshape(DEPTH * N_EXPERTS, D),
        "positions": np.ascontiguousarray(a["positions_2"]),
    }


def kernel(**inputs):
    import concourse.bacc as _bacc
    from concourse.bass_utils import run_bass_kernel_spmd as _run

    arrays = lay_out(inputs)
    nc = _bacc.Bacc("TRN2", target_bir_lowering=False, num_devices=1)
    io = {n: nc.dram_tensor(f"in_{n}_dram", a.shape, mybir.dt.from_np(a.dtype), kind="ExternalInput").ap()
          for n, a in arrays.items()}
    io["out"] = nc.dram_tensor("out_0_dram", (P, KD, S), F32, kind="ExternalOutput").ap()
    program(nc, io)
    r = _run(nc, [{f"in_{n}_dram": a for n, a in arrays.items()}], core_ids=[0])
    out = r.results[0]["out_0_dram"]
    return np.ascontiguousarray(out.transpose(2, 1, 0).reshape(1, S, D))
```
